# Optimizing a Trainium2 kernel written in Bass

```python
import math
import jax
import jax.numpy as jnp
from jax import lax
import numpy as np
import jax, jax.numpy as jnp

D_MODEL = 1024
BATCH = 1
SEQ = 256
DEPTH = 4

N_MIXERS = 3
N_SUB = 3
NORM_EPS = 1e-6
D_FF = 2816
MACARON_W = 0.5
N_A = (DEPTH + 2) // 3
N_B = (DEPTH + 1) // 3
N_C = DEPTH // 3
N_A_VRES = max(N_A - 1, 0)

RW_HEAD = 64
RW_HEADS = D_MODEL // RW_HEAD
RW_DECAY_LORA = max(32, int(round(1.8 * D_MODEL ** 0.5 / 32)) * 32)
RW_AAA_LORA = max(32, int(round(1.8 * D_MODEL ** 0.5 / 32)) * 32)
RW_MV_LORA = max(32, int(round(1.3 * D_MODEL ** 0.5 / 32)) * 32)
RW_GATE_LORA = max(32, int(round(0.6 * D_MODEL ** 0.8 / 32)) * 32)
RW_GN_EPS = 64e-5

MB_D_INNER = 2 * D_MODEL
MB_HEADDIM = 64
MB_HEADS = MB_D_INNER // MB_HEADDIM
MB_GROUPS = 8
MB_STATE = 128
MB_CONV = 4
MB_CHUNK = 128
MB_CONV_DIM = MB_D_INNER + 2 * MB_GROUPS * MB_STATE
MB_IN_DIM = MB_D_INNER + MB_CONV_DIM + MB_HEADS

SW_HEAD_DIM = 64
SW_Q_HEADS = D_MODEL // SW_HEAD_DIM
SW_KV_HEADS = 4
SW_WINDOW = 128
SW_BLOCK = 128
NEG_INF = -1e30


def rms_norm(x, g, eps=NORM_EPS):
    xf = x.astype(jnp.float32)
    y = xf * lax.rsqrt(jnp.mean(xf * xf, axis=-1, keepdims=True) + eps)
    return (y * g.astype(jnp.float32)).astype(x.dtype)

def adaln(x, g, shift, scale):
    return rms_norm(x, g) * (1 + scale[:, None, :]) + shift[:, None, :]

def swiglu(h, w_in, w_out):
    a, b = jnp.split(h @ w_in, 2, axis=-1)
    return (jax.nn.silu(a) * b) @ w_out

def token_shift(h):
    return jnp.pad(h, ((0, 0), (1, 0), (0, 0)))[:, :-1]

def rwkv7_time_mix(h, mu, w_rkv, w_o, w0, w1, w2, a0, a1, a2, g1, g2,
                   k_k, k_a, r_k, ln_w, ln_b, v_first, vres):
    f32 = jnp.float32
    bsz, seq, d = h.shape
    H, N = RW_HEADS, RW_HEAD
    dx = token_shift(h) - h
    xr, xw, xk, xv, xa, xg = [h + dx * mu[j] for j in range(6)]
    r = xr @ w_rkv[0]
    k = xk @ w_rkv[1]
    v = xv @ w_rkv[2]
    w = -jax.nn.softplus(-(w0 + jnp.tanh(xw @ w1) @ w2)) - 0.5
    decay = jnp.exp(-jnp.exp(w.astype(f32)))
    a = jax.nn.sigmoid(a0 + (xa @ a1) @ a2)
    if vres is None:
        v_first = v
    else:
        v0, v1, v2 = vres
        v = v + (v_first - v) * jax.nn.sigmoid(v0 + (xv @ v1) @ v2)
    g = jax.nn.sigmoid(xg @ g1) @ g2

    def heads(t):
        return t.reshape(bsz, seq, H, N).astype(f32)

    kk = heads(k * k_k)
    kk = kk / jnp.maximum(jnp.sqrt(jnp.sum(kk * kk, axis=-1, keepdims=True)), 1e-12)
    k = k * (1 + (a - 1) * k_a)
    rh, kh, vh, wh, ah = heads(r), heads(k), heads(v), heads(decay), heads(a)

    def step(state, inp):
        r_t, w_t, k_t, v_t, kk_t, a_t = inp
        sa = jnp.einsum('bhvk,bhk->bhv', state, -kk_t)
        state = (state * w_t[:, :, None, :]
                 + sa[..., None] * (kk_t * a_t)[:, :, None, :]
                 + v_t[..., None] * k_t[:, :, None, :])
        return state, jnp.einsum('bhvk,bhk->bhv', state, r_t)

    def tm(t):
        return jnp.swapaxes(t, 0, 1)

    state0 = jnp.zeros((bsz, H, N, N), f32)
    _, y = lax.scan(step, state0, (tm(rh), tm(wh), tm(kh), tm(vh), tm(kk), tm(ah)))
    y = tm(y)
    mean = jnp.mean(y, axis=-1, keepdims=True)
    var = jnp.mean(jnp.square(y - mean), axis=-1, keepdims=True)
    y = ((y - mean) * lax.rsqrt(var + RW_GN_EPS)).reshape(bsz, seq, d) * ln_w + ln_b
    bonus = jnp.sum(rh * kh * r_k, axis=-1, keepdims=True) * vh
    out = ((y + bonus.reshape(bsz, seq, d)) * g).astype(h.dtype) @ w_o
    return out, v_first

def causal_dwconv(x, w, b):
    k_w, ch = w.shape
    out = lax.conv_general_dilated(x, w[:, None, :].astype(x.dtype), window_strides=(1,),
                                   padding=[(k_w - 1, 0)],
                                   dimension_numbers=('NWC', 'WIO', 'NWC'),
                                   feature_group_count=ch)
    return out + b

def ssd_chunked(x, dt, A, Bm, Cm):
    f32 = jnp.float32
    bsz, seq, H, P = x.shape
    G, N = Bm.shape[2], Bm.shape[3]
    hg = H // G
    L = MB_CHUNK
    nc = seq // L
    X = (x.astype(f32) * dt[..., None]).reshape(bsz, nc, L, G, hg, P)
    dA = (dt * A).reshape(bsz, nc, L, G, hg)
    Bc = Bm.astype(f32).reshape(bsz, nc, L, G, N)
    Cc = Cm.astype(f32).reshape(bsz, nc, L, G, N)
    X, dA, Bc, Cc = [jnp.moveaxis(t, 1, 0) for t in (X, dA, Bc, Cc)]
    mask = jnp.tril(jnp.ones((L, L), dtype=bool))[None, :, :, None, None]

    def step(state, inp):
        Xc, dAc, Bk, Ck = inp
        acum = jnp.cumsum(dAc, axis=1)
        seg = acum[:, :, None] - acum[:, None, :]
        lmat = jnp.exp(jnp.where(mask, seg, -jnp.inf))
        cb = jnp.einsum('blgn,bsgn->blsg', Ck, Bk)
        y_diag = jnp.einsum('blsgh,bsghp->blghp', cb[..., None] * lmat, Xc)
        y_off = jnp.einsum('blgn,bghpn->blghp', Ck, state) * jnp.exp(acum)[..., None]
        decay_end = jnp.exp(acum[:, -1:] - acum)
        new_state = (state * jnp.exp(acum[:, -1])[..., None, None]
                     + jnp.einsum('blgn,blghp->bghpn', Bk, Xc * decay_end[..., None]))
        return new_state, y_diag + y_off

    state0 = jnp.zeros((bsz, G, hg, P, N), f32)
    _, y = lax.scan(step, state0, (X, dA, Bc, Cc))
    return jnp.moveaxis(y, 0, 1).reshape(bsz, seq, H, P)

def mamba2_ssd_mix(h, w_in, conv_w, conv_b, dt_bias, A_log, D_skip, norm_g, w_out):
    f32 = jnp.float32
    bsz, seq, _ = h.shape
    zxbcdt = h @ w_in
    z, xbc, dt = jnp.split(zxbcdt, [MB_D_INNER, MB_D_INNER + MB_CONV_DIM], axis=-1)
    xbc = jax.nn.silu(causal_dwconv(xbc, conv_w, conv_b))
    xs, Bm, Cm = jnp.split(xbc, [MB_D_INNER, MB_D_INNER + MB_GROUPS * MB_STATE], axis=-1)
    dt = jax.nn.softplus((dt + dt_bias).astype(f32))
    A = -jnp.exp(A_log.astype(f32))
    xs = xs.reshape(bsz, seq, MB_HEADS, MB_HEADDIM)
    y = ssd_chunked(xs, dt, A,
                    Bm.reshape(bsz, seq, MB_GROUPS, MB_STATE),
                    Cm.reshape(bsz, seq, MB_GROUPS, MB_STATE))
    y = y + xs.astype(f32) * D_skip.astype(f32)[:, None]
    y = y.reshape(bsz, seq, MB_D_INNER) * jax.nn.silu(z.astype(f32))
    y = rms_norm(y.reshape(bsz, seq, MB_GROUPS, -1), norm_g.reshape(MB_GROUPS, -1))
    return y.reshape(bsz, seq, MB_D_INNER).astype(h.dtype) @ w_out

def swa_sink_attention(h, w_qkv, q_norm, k_norm, sinks, w_o):
    f32 = jnp.float32
    bsz, seq, _ = h.shape
    Hq, Hk, Dh, T = SW_Q_HEADS, SW_KV_HEADS, SW_HEAD_DIM, SW_BLOCK
    G = Hq // Hk
    nb = seq // T
    q, k, v = jnp.split(h @ w_qkv, [Hq * Dh, (Hq + Hk) * Dh], axis=-1)
    q = rms_norm(q.reshape(bsz, seq, Hq, Dh), q_norm).reshape(bsz, nb, T, Hk, G, Dh)
    k = rms_norm(k.reshape(bsz, seq, Hk, Dh), k_norm).reshape(bsz, nb, T, Hk, Dh)
    v = v.reshape(bsz, nb, T, Hk, Dh)

    def with_prev(t):
        prev = jnp.pad(t, ((0, 0), (1, 0), (0, 0), (0, 0), (0, 0)))[:, :-1]
        return jnp.concatenate([prev, t], axis=2)

    kb, vb = with_prev(k), with_prev(v)
    qi = jnp.arange(T)[:, None]
    si = jnp.arange(2 * T)[None, :]
    rel = qi + T - si
    band = (rel >= 0) & (rel < SW_WINDOW)
    mask = band[None] & ((jnp.arange(nb)[:, None, None] > 0) | (si >= T)[None])
    scale = Dh ** -0.5
    sink = sinks.astype(f32).reshape(Hk, G)[None, :, :, None, None]

    def block(args):
        qb, kbb, vbb, mb = args
        s = jnp.einsum('bqkgd,bskd->bkgqs', qb, kbb).astype(f32) * scale
        s = jnp.where(mb, s, NEG_INF)
        m = jnp.maximum(jnp.max(s, axis=-1, keepdims=True), sink)
        p = jnp.exp(s - m)
        denom = jnp.sum(p, axis=-1, keepdims=True) + jnp.exp(sink - m)
        return jnp.einsum('bkgqs,bskd->bqkgd', (p / denom).astype(vbb.dtype), vbb)

    o = lax.map(block, (jnp.moveaxis(q, 1, 0), jnp.moveaxis(kb, 1, 0),
                        jnp.moveaxis(vb, 1, 0), mask))
    o = jnp.moveaxis(o, 0, 1).reshape(bsz, seq, Hq * Dh)
    return o @ w_o

def first_inputs(seed: int = 0) -> dict:
    key = jax.random.key(seed)
    ks = iter(jax.random.split(key, 64))

    def nrm(shape, scale=1.0):
        return scale * jax.random.normal(next(ks), shape, jnp.float32)

    def unif(shape, lo, hi):
        return jax.random.uniform(next(ks), shape, jnp.float32, lo, hi)

    D = D_MODEL
    dt0 = jnp.exp(unif((N_B, MB_HEADS), math.log(1e-3), math.log(1e-1)))
    return {
        'x': nrm((BATCH, SEQ, D)),
        'c': nrm((BATCH, D)),
        'ada_w': nrm((DEPTH, D, N_SUB * 3 * D), 0.5 * D ** -0.5),
        'ada_b': nrm((DEPTH, N_SUB * 3 * D), 0.02),
        'norm_g': 1.0 + nrm((DEPTH, N_SUB, D), 0.05),
        'ffn_w_in': nrm((DEPTH, 2, D, 2 * D_FF), D ** -0.5),
        'ffn_w_out': nrm((DEPTH, 2, D_FF, D), D_FF ** -0.5),
        'rw_mu': unif((N_A, 6, D), 0.0, 1.0),
        'rw_w_rkv': nrm((N_A, 3, D, D), D ** -0.5),
        'rw_w_o': nrm((N_A, D, D), D ** -0.5),
        'rw_w0': unif((N_A, D), -6.5, -1.5),
        'rw_w1': nrm((N_A, D, RW_DECAY_LORA), D ** -0.5),
        'rw_w2': nrm((N_A, RW_DECAY_LORA, D), 0.1 * RW_DECAY_LORA ** -0.5),
        'rw_a0': nrm((N_A, D), 0.1),
        'rw_a1': nrm((N_A, D, RW_AAA_LORA), D ** -0.5),
        'rw_a2': nrm((N_A, RW_AAA_LORA, D), 0.5 * RW_AAA_LORA ** -0.5),
        'rw_g1': nrm((N_A, D, RW_GATE_LORA), D ** -0.5),
        'rw_g2': nrm((N_A, RW_GATE_LORA, D), RW_GATE_LORA ** -0.5),
        'rw_k_k': 0.85 + nrm((N_A, D), 0.05),
        'rw_k_a': 1.0 + nrm((N_A, D), 0.05),
        'rw_r_k': nrm((N_A, RW_HEADS, RW_HEAD), 0.1),
        'rw_ln_w': 1.0 + nrm((N_A, D), 0.05),
        'rw_ln_b': nrm((N_A, D), 0.02),
        'rw_v0': 1.0 + nrm((N_A_VRES, D), 0.1),
        'rw_v1': nrm((N_A_VRES, D, RW_MV_LORA), D ** -0.5),
        'rw_v2': nrm((N_A_VRES, RW_MV_LORA, D), 0.5 * RW_MV_LORA ** -0.5),
        'mb_w_in': nrm((N_B, D, MB_IN_DIM), D ** -0.5),
        'mb_conv_w': nrm((N_B, MB_CONV, MB_CONV_DIM), 0.5),
        'mb_conv_b': nrm((N_B, MB_CONV_DIM), 0.02),
        'mb_dt_bias': dt0 + jnp.log(-jnp.expm1(-dt0)),
        'mb_A_log': jnp.log(unif((N_B, MB_HEADS), 1.0, 16.0)),
        'mb_D': 1.0 + nrm((N_B, MB_HEADS), 0.1),
        'mb_norm_g': 1.0 + nrm((N_B, MB_D_INNER), 0.05),
        'mb_w_out': nrm((N_B, MB_D_INNER, D), MB_D_INNER ** -0.5),
        'sw_w_qkv': nrm((N_C, D, (SW_Q_HEADS + 2 * SW_KV_HEADS) * SW_HEAD_DIM), D ** -0.5),
        'sw_q_norm': 1.0 + nrm((N_C, SW_HEAD_DIM), 0.05),
        'sw_k_norm': 1.0 + nrm((N_C, SW_HEAD_DIM), 0.05),
        'sw_sinks': nrm((N_C, SW_Q_HEADS), 0.5),
        'sw_w_o': nrm((N_C, SW_Q_HEADS * SW_HEAD_DIM, D), (SW_Q_HEADS * SW_HEAD_DIM) ** -0.5),
    }

def first_block(x, c, ada_w, ada_b, norm_g, ffn_w_in, ffn_w_out,
              rw_mu, rw_w_rkv, rw_w_o, rw_w0, rw_w1, rw_w2, rw_a0, rw_a1, rw_a2,
              rw_g1, rw_g2, rw_k_k, rw_k_a, rw_r_k, rw_ln_w, rw_ln_b,
              rw_v0, rw_v1, rw_v2,
              mb_w_in, mb_conv_w, mb_conv_b, mb_dt_bias, mb_A_log, mb_D, mb_norm_g, mb_w_out,
              sw_w_qkv, sw_q_norm, sw_k_norm, sw_sinks, sw_w_o):
    bsz, _, d = x.shape
    c_act = jax.nn.silu(c)
    v_first = None
    for i in range(DEPTH):
        mod = (c_act @ ada_w[i] + ada_b[i]).reshape(bsz, N_SUB, 3, d)
        shift, scale, gate = mod[:, :, 0], mod[:, :, 1], mod[:, :, 2]

        h = adaln(x, norm_g[i, 0], shift[:, 0], scale[:, 0])
        x = x + MACARON_W * gate[:, 0, None] * swiglu(h, ffn_w_in[i, 0], ffn_w_out[i, 0])

        h = adaln(x, norm_g[i, 1], shift[:, 1], scale[:, 1])
        kind, j = i % N_MIXERS, i // N_MIXERS
        if kind == 0:
            vres = None if v_first is None else (rw_v0[j - 1], rw_v1[j - 1], rw_v2[j - 1])
            y, v_first = rwkv7_time_mix(h, rw_mu[j], rw_w_rkv[j], rw_w_o[j], rw_w0[j], rw_w1[j],
                                        rw_w2[j], rw_a0[j], rw_a1[j], rw_a2[j], rw_g1[j],
                                        rw_g2[j], rw_k_k[j], rw_k_a[j], rw_r_k[j],
                                        rw_ln_w[j], rw_ln_b[j], v_first, vres)
        elif kind == 1:
            y = mamba2_ssd_mix(h, mb_w_in[j], mb_conv_w[j], mb_conv_b[j], mb_dt_bias[j],
                               mb_A_log[j], mb_D[j], mb_norm_g[j], mb_w_out[j])
        else:
            y = swa_sink_attention(h, sw_w_qkv[j], sw_q_norm[j], sw_k_norm[j],
                                   sw_sinks[j], sw_w_o[j])
        x = x + gate[:, 1, None] * y

        h = adaln(x, norm_g[i, 2], shift[:, 2], scale[:, 2])
        x = x + MACARON_W * gate[:, 2, None] * swiglu(h, ffn_w_in[i, 1], ffn_w_out[i, 1])
    return x


DEPTH_2 = 1

D_RNN = 1024
N_LRU_BLOCKS = 16
LRU_BLOCK = D_RNN // N_LRU_BLOCKS
CONV_WIDTH = 4
LRU_C = 8.0
ATTN_GROUPS = ((128, 1), (512, 4), (2048, 16))
N_GROUPS = len(ATTN_GROUPS)
HEADS_PER_GROUP = 4
HEAD_DIM = 128
ATTN_WIDTH = N_GROUPS * HEADS_PER_GROUP * HEAD_DIM
ATTN_OUT_WIDTH = HEADS_PER_GROUP * HEAD_DIM
ROPE_DIM = HEAD_DIM // 4
ROPE_THETA = 500000.0
Q_BLOCK = 128
N_BRANCHES = 2
D_FF_2 = ((8 * D_MODEL // 3 + 255) // 256) * 256
IN_WIDTH = 2 * D_RNN + 3 * ATTN_WIDTH + N_BRANCHES * D_MODEL
EPS = 1e-6
NEG = -1e30


def rms_norm_2(x, g):
    xf = x.astype(jnp.float32)
    y = xf * lax.rsqrt(jnp.mean(xf * xf, axis=-1, keepdims=True) + EPS)
    return (y * g.astype(jnp.float32)).astype(x.dtype)

def causal_depthwise_conv(x, w, b):
    y = lax.conv_general_dilated(
        x, w[:, None, :].astype(x.dtype), window_strides=(1,),
        padding=((CONV_WIDTH - 1, 0),), dimension_numbers=('NWC', 'WIO', 'NWC'),
        feature_group_count=x.shape[-1])
    return y + b.astype(x.dtype)

def rg_lru(x, w_rg, b_rg, w_ig, b_ig, lam):
    B, S, _ = x.shape
    xf = x.astype(jnp.float32)
    xb = xf.reshape(B, S, N_LRU_BLOCKS, LRU_BLOCK)
    r = jax.nn.sigmoid(jnp.einsum('bsnc,ncd->bsnd', xb, w_rg.astype(jnp.float32)).reshape(B, S, D_RNN) + b_rg.astype(jnp.float32))
    i = jax.nn.sigmoid(jnp.einsum('bsnc,ncd->bsnd', xb, w_ig.astype(jnp.float32)).reshape(B, S, D_RNN) + b_ig.astype(jnp.float32))
    log_a = -LRU_C * r * jax.nn.softplus(-lam.astype(jnp.float32))
    a = jnp.exp(log_a)
    mult = jnp.sqrt(-jnp.expm1(2.0 * log_a))
    mult = jnp.where(jnp.arange(S)[None, :, None] == 0, 1.0, mult)
    u = mult * (i * xf)

    def combine(left, right):
        a1, b1 = left
        a2, b2 = right
        return a1 * a2, a2 * b1 + b2

    _, h = lax.associative_scan(combine, (a, u), axis=1)
    return h.astype(x.dtype)

def partial_rope(t, cos, sin):
    half = ROPE_DIM // 2
    t1 = t[..., :half]
    t2 = t[..., half:ROPE_DIM]
    return jnp.concatenate([t1 * cos - t2 * sin, t2 * cos + t1 * sin, t[..., ROPE_DIM:]], axis=-1)

def dilated_window_attention(q, k, v, window, dilation):
    B, S, H, Dh = q.shape
    w_sub = window // dilation
    L = -(-S // dilation)
    nb = -(-L // Q_BLOCK)
    Lp = nb * Q_BLOCK
    pad = Lp * dilation - S

    def to_blocks(t):
        t = jnp.pad(t.astype(jnp.float32), ((0, 0), (0, pad), (0, 0), (0, 0)))
        t = t.reshape(B, Lp, dilation, H, Dh).transpose(0, 2, 1, 3, 4)
        return t.reshape(B, dilation, nb, Q_BLOCK, H, Dh)

    def with_prev(t):
        prev = jnp.pad(t[:, :, :-1], ((0, 0), (0, 0), (1, 0), (0, 0), (0, 0), (0, 0)))
        return jnp.concatenate([prev, t], axis=3)

    qb = to_blocks(q)
    kb = with_prev(to_blocks(k))
    vb = with_prev(to_blocks(v))

    qi = jnp.arange(Q_BLOCK)[:, None]
    kj = jnp.arange(2 * Q_BLOCK)[None, :]
    diff = qi + Q_BLOCK - kj
    band = (diff >= 0) & (diff <= w_sub)
    has_prev = (jnp.arange(nb)[:, None, None] > 0) | (kj[None] >= Q_BLOCK)
    mask = band[None] & has_prev

    s = jnp.einsum('brnqhc,brnkhc->brnhqk', qb, kb)
    s = jnp.where(mask[None, None, :, None], s, NEG)
    m = jnp.max(s, axis=-1, keepdims=True)
    p = jnp.exp(s - m)
    den = jnp.sum(p, axis=-1, keepdims=True)
    o = jnp.einsum('brnhqk,brnkhc->brnqhc', p, vb) / jnp.swapaxes(den, 3, 4)
    lse = jnp.swapaxes((m + jnp.log(den))[..., 0], 3, 4)

    o = o.reshape(B, dilation, Lp, H, Dh).transpose(0, 2, 1, 3, 4).reshape(B, Lp * dilation, H, Dh)[:, :S]
    lse = lse.reshape(B, dilation, Lp, H).transpose(0, 2, 1, 3).reshape(B, Lp * dilation, H)[:, :S]
    return o, lse

def second_inputs(seed: int = 0) -> dict:
    key = jax.random.key(seed)
    ks = jax.random.split(key, 24)
    f32 = jnp.float32

    def nrm(k, shape, fan_in):
        return jax.random.normal(k, shape, f32) * (fan_in ** -0.5)

    def gain(k):
        return 1.0 + 0.02 * jax.random.normal(k, (DEPTH_2, D_MODEL), f32)

    x = jax.random.normal(ks[0], (BATCH, SEQ, D_MODEL), f32)
    offset = jax.random.randint(ks[1], (BATCH, 1), 0, 4096, dtype=jnp.int32)
    positions = offset + jnp.arange(SEQ, dtype=jnp.int32)[None, :]
    u = jax.random.uniform(ks[2], (DEPTH_2, D_RNN), f32, 0.9, 0.999)
    a_base = u ** (1.0 / LRU_C)
    lru_lambda = jnp.log(a_base) - jnp.log1p(-a_base)
    return {
        "x": x,
        "positions": positions,
        "pre_mix_norm": gain(ks[3]),
        "w_in": nrm(ks[4], (DEPTH_2, D_MODEL, IN_WIDTH), D_MODEL),
        "conv_w": nrm(ks[5], (DEPTH_2, CONV_WIDTH, D_RNN), CONV_WIDTH),
        "conv_b": 0.01 * jax.random.normal(ks[6], (DEPTH_2, D_RNN), f32),
        "w_rg": nrm(ks[7], (DEPTH_2, N_LRU_BLOCKS, LRU_BLOCK, LRU_BLOCK), LRU_BLOCK),
        "b_rg": 0.01 * jax.random.normal(ks[8], (DEPTH_2, D_RNN), f32),
        "w_ig": nrm(ks[9], (DEPTH_2, N_LRU_BLOCKS, LRU_BLOCK, LRU_BLOCK), LRU_BLOCK),
        "b_ig": 0.01 * jax.random.normal(ks[10], (DEPTH_2, D_RNN), f32),
        "lru_lambda": lru_lambda,
        "w_lru_proj": nrm(ks[11], (DEPTH_2, D_RNN, D_MODEL), D_RNN),
        "w_attn_proj": nrm(ks[12], (DEPTH_2, ATTN_OUT_WIDTH, D_MODEL), ATTN_OUT_WIDTH),
        "w_out": nrm(ks[13], (DEPTH_2, D_MODEL, D_MODEL), D_MODEL),
        "post_mix_norm": gain(ks[14]),
        "pre_ffn_norm": gain(ks[15]),
        "w_ffn_gate": nrm(ks[16], (DEPTH_2, D_MODEL, D_FF_2), D_MODEL),
        "w_ffn_up": nrm(ks[17], (DEPTH_2, D_MODEL, D_FF_2), D_MODEL),
        "w_ffn_down": nrm(ks[18], (DEPTH_2, D_FF_2, D_MODEL), D_FF_2),
        "post_ffn_norm": gain(ks[19]),
    }

def second_block(x, positions, pre_mix_norm, w_in, conv_w, conv_b, w_rg, b_rg, w_ig, b_ig,
              lru_lambda, w_lru_proj, w_attn_proj, w_out, post_mix_norm, pre_ffn_norm,
              w_ffn_gate, w_ffn_up, w_ffn_down, post_ffn_norm):
    B, S, _ = x.shape
    dt = x.dtype
    inv_freq = ROPE_THETA ** (-jnp.arange(0, ROPE_DIM, 2, dtype=jnp.float32) / ROPE_DIM)
    ang = positions.astype(jnp.float32)[..., None] * inv_freq
    cos = jnp.cos(ang)[:, :, None, :].astype(dt)
    sin = jnp.sin(ang)[:, :, None, :].astype(dt)
    split_at = np.cumsum([D_RNN, D_RNN, ATTN_WIDTH, ATTN_WIDTH, ATTN_WIDTH]).tolist()

    for l in range(DEPTH_2):
        h = rms_norm_2(x, pre_mix_norm[l])
        proj = h @ w_in[l].astype(dt)
        xr, gr, q, k, v, gates = jnp.split(proj, split_at, axis=-1)

        xr = causal_depthwise_conv(xr, conv_w[l], conv_b[l])
        xr = rg_lru(xr, w_rg[l], b_rg[l], w_ig[l], b_ig[l], lru_lambda[l])
        y_lru = (xr * jax.nn.gelu(gr)) @ w_lru_proj[l].astype(dt)

        q = q.reshape(B, S, N_GROUPS, HEADS_PER_GROUP, HEAD_DIM)
        k = k.reshape(B, S, N_GROUPS, HEADS_PER_GROUP, HEAD_DIM)
        v = v.reshape(B, S, N_GROUPS, HEADS_PER_GROUP, HEAD_DIM)
        q = partial_rope(q, cos[:, :, None], sin[:, :, None]) * (HEAD_DIM ** -0.5)
        k = partial_rope(k, cos[:, :, None], sin[:, :, None])
        outs, lses = [], []
        for g, (window, dilation) in enumerate(ATTN_GROUPS):
            o_g, lse_g = dilated_window_attention(q[:, :, g], k[:, :, g], v[:, :, g], window, dilation)
            outs.append(o_g)
            lses.append(lse_g)
        o = jnp.stack(outs, axis=2)
        wts = jax.nn.softmax(jnp.stack(lses, axis=2), axis=2)
        o = jnp.sum(wts[..., None] * o, axis=2).reshape(B, S, ATTN_OUT_WIDTH).astype(dt)
        y_attn = o @ w_attn_proj[l].astype(dt)

        g_lru, g_attn = jnp.split(jax.nn.sigmoid(gates), N_BRANCHES, axis=-1)
        mix = (g_lru * y_lru + g_attn * y_attn) @ w_out[l].astype(dt)
        x = x + rms_norm_2(mix, post_mix_norm[l])

        h = rms_norm_2(x, pre_ffn_norm[l])
        f = (jax.nn.silu(h @ w_ffn_gate[l].astype(dt)) * (h @ w_ffn_up[l].astype(dt))) @ w_ffn_down[l].astype(dt)
        x = x + rms_norm_2(f, post_ffn_norm[l])
    return x


def setup_inputs(seed=0):
    out = dict(first_inputs(seed))
    for name, value in second_inputs(seed + 1).items():
        if name != "x":
            out[name + "_2"] = value
    return out


def reference(
    x, c, ada_w, ada_b, norm_g, ffn_w_in, ffn_w_out, rw_mu, rw_w_rkv, rw_w_o, rw_w0, rw_w1,
    rw_w2, rw_a0, rw_a1, rw_a2, rw_g1, rw_g2, rw_k_k, rw_k_a, rw_r_k, rw_ln_w, rw_ln_b, rw_v0,
    rw_v1, rw_v2, mb_w_in, mb_conv_w, mb_conv_b, mb_dt_bias, mb_A_log, mb_D, mb_norm_g,
    mb_w_out, sw_w_qkv, sw_q_norm, sw_k_norm, sw_sinks, sw_w_o, positions_2, pre_mix_norm_2,
    w_in_2, conv_w_2, conv_b_2, w_rg_2, b_rg_2, w_ig_2, b_ig_2, lru_lambda_2, w_lru_proj_2,
    w_attn_proj_2, w_out_2, post_mix_norm_2, pre_ffn_norm_2, w_ffn_gate_2, w_ffn_up_2,
    w_ffn_down_2, post_ffn_norm_2,
):
    x = first_block(
        x, c, ada_w, ada_b, norm_g, ffn_w_in, ffn_w_out, rw_mu, rw_w_rkv, rw_w_o, rw_w0, rw_w1,
        rw_w2, rw_a0, rw_a1, rw_a2, rw_g1, rw_g2, rw_k_k, rw_k_a, rw_r_k, rw_ln_w, rw_ln_b,
        rw_v0, rw_v1, rw_v2, mb_w_in, mb_conv_w, mb_conv_b, mb_dt_bias, mb_A_log, mb_D,
        mb_norm_g, mb_w_out, sw_w_qkv, sw_q_norm, sw_k_norm, sw_sinks, sw_w_o,
    )
    return second_block(
        x, positions_2, pre_mix_norm_2, w_in_2, conv_w_2, conv_b_2, w_rg_2, b_rg_2, w_ig_2,
        b_ig_2, lru_lambda_2, w_lru_proj_2, w_attn_proj_2, w_out_2, post_mix_norm_2,
        pre_ffn_norm_2, w_ffn_gate_2, w_ffn_up_2, w_ffn_down_2, post_ffn_norm_2,
    )


_drawn_inputs = setup_inputs


def setup_inputs(seed=0):
    import zlib

    import numpy as np

    out = dict(_drawn_inputs(seed))
    spreads = {}
    factors = {'rw_w1': 8.0,
     'rw_w2': 8.0,
     'rw_a0': 2.838,
     'rw_ln_w': 2.993,
     'rw_ln_b': 3.74,
     'rw_v0': 54.352,
     'mb_conv_b': 3.869,
     'sw_q_norm': 8.0,
     'sw_k_norm': 8.0,
     'sw_sinks': 49.065,
     'b_rg_2': 29.619,
     'b_ig_2': 8.0,
     'post_mix_norm_2': 3.747,
     'pre_ffn_norm_2': 3.617,
     'post_ffn_norm_2': 42.474,
     'rw_v1': 8.0,
     'rw_v2': 8.0}
    for name, (base, spread) in spreads.items():
        noise = np.random.default_rng([zlib.crc32(name.encode()), seed]).standard_normal(out[name].shape)
        drawn = base * np.exp(spread * noise) if base else spread * noise
        out[name] = jnp.asarray(drawn.astype(out[name].dtype))
    for name, factor in factors.items():
        out[name] = (out[name] * factor).astype(out[name].dtype)
    return out
```

```python
import numpy as np
import concourse.bass as bass
from concourse import mybir
from contextlib import ExitStack

FP32 = mybir.dt.float32
FP32R = mybir.dt.float32r
INT32 = mybir.dt.int32
ALU = mybir.AluOpType
ACT = mybir.ActivationFunctionType
AX = mybir.AxisListType

P = 128
T = 256
D = 1024
KT = D // P
F = 2816
FT = F // P
DEPTH = 4
BLOCKS = 24
RING = 3
EPS = 1e-6
NORMS = 3 * DEPTH
ADA_COLS = 3 * D
ADA_CHUNK = 256
ADA_STEPS = ADA_COLS // ADA_CHUNK
FFN_SLOTS = FT
FFN_PEELED = 3
FFN_UNROLL = 6
RW_SLOTS, MB_SLOTS, SW_SLOTS, B2_SLOTS = 14, 22, 7, 30
STAGES = 12
B2_TOTAL = 52
UPDATES = STAGES + 2



def blocks_of(w):
    k, n = w.shape
    kt, nt = -(-k // P), -(-n // P)
    full = np.zeros((kt * P, nt * P), w.dtype)
    full[:k, :n] = w
    return full.reshape(kt, P, nt, P).transpose(2, 0, 1, 3)


def moving_blocks(w, width):
    k, n = w.shape
    b = w.reshape(k // P, P, n // width, width // P, P)
    return b.transpose(2, 0, 3, 1, 4).reshape(-1, P, P)


def slots_of(parts):
    b = np.concatenate([p.reshape(-1, P, P) for p in parts])
    pad = -len(b) % BLOCKS
    b = np.concatenate([b, np.zeros((pad, P, P), b.dtype)])
    return b.reshape(-1, BLOCKS, P, P).transpose(0, 2, 1, 3).reshape(-1, P, BLOCKS * P)


def ffn_slots(w_a, w_b, w_out):
    a, b, o = blocks_of(w_a), blocks_of(w_b), blocks_of(w_out)
    parts = []
    for f in range(FT):
        parts += [a[f], b[f], o[:, f]]
    return slots_of(parts)


def weight_slots(v):
    out = [slots_of([blocks_of(v["ada_w"][0][:, :ADA_COLS])])]
    for i in range(DEPTH):
        kind, j = i % 3, i // 3
        for s in range(2):
            if s == 1:
                if kind == 0:
                    w_r, w_k, w_v = v["rw_w_rkv"][j]
                    parts = [blocks_of(w_k)]
                    parts += [blocks_of(v[n][j]) for n in ("rw_w1", "rw_a1", "rw_w2", "rw_a2")]
                    parts += [blocks_of(w_r), blocks_of(w_v)]
                    if j:
                        parts.append(blocks_of(v["rw_v1"][j - 1]))
                    parts.append(blocks_of(v["rw_g1"][j]))
                    if j:
                        parts.append(blocks_of(v["rw_v2"][j - 1]))
                    parts += [blocks_of(v["rw_g2"][j]), blocks_of(v["rw_w_o"][j])]
                elif kind == 1:
                    parts = [blocks_of(v["mb_w_in"][j]), blocks_of(v["mb_w_out"][j])]
                else:
                    w = v["sw_w_qkv"][j]
                    parts = [blocks_of(w[:, :1280]), moving_blocks(w[:, 1280:], 256), blocks_of(v["sw_w_o"][j])]
                out.append(slots_of(parts))
            w = v["ffn_w_in"][i, s]
            out.append(ffn_slots(w[:, :F], w[:, F:], v["ffn_w_out"][i, s]))
    w = v["w_in_2"][0]
    diag = []
    for name in ("w_rg_2", "w_ig_2"):
        g = v[name][0]
        b = np.zeros((KT, P, P), g.dtype)
        b[:, :64, :64] = g[0::2]
        b[:, 64:, 64:] = g[1::2]
        diag.append(b)
    out.append(slots_of([blocks_of(w[:, :5120]), moving_blocks(w[:, 5120:6656], 512), diag[0], diag[1],
                         blocks_of(w[:, 6656:]), blocks_of(v["w_lru_proj_2"][0]),
                         blocks_of(v["w_attn_proj_2"][0]), blocks_of(v["w_out_2"][0])]))
    out.append(ffn_slots(v["w_ffn_gate_2"][0], v["w_ffn_up_2"][0], v["w_ffn_down_2"][0]))
    out.append(np.zeros_like(out[0][:-sum(len(o) for o in out) % RING]))
    return np.concatenate(out)


def columns(a):
    a = np.asarray(a)
    return a.reshape(-1, P).T


def param_parts(v):
    parts = {"c": columns(v["c"]), "norm_g": columns(v["norm_g"]), "ada_b": columns(v["ada_b"])}
    for j in range(2):
        for n in ("rw_mu", "rw_w0", "rw_a0", "rw_k_k", "rw_k_a", "rw_r_k", "rw_ln_w", "rw_ln_b"):
            parts[f"{n}{j}"] = columns(v[n][j])
    parts["rw_v0"] = columns(v["rw_v0"][0])
    parts["mb_conv_w"] = columns(v["mb_conv_w"][0])
    parts["mb_conv_b"] = columns(v["mb_conv_b"][0])
    for n in ("mb_dt_bias", "mb_A_log"):
        col = np.zeros((P, 1), v[n].dtype)
        col[:32, 0] = v[n][0]
        parts[n] = col
    parts["mb_D"] = columns(np.repeat(v["mb_D"][0], 64))
    parts["mb_norm_g"] = columns(v["mb_norm_g"][0])
    parts["sw_q_norm"] = columns(np.tile(v["sw_q_norm"][0], 2))
    parts["sw_k_norm"] = columns(np.tile(v["sw_k_norm"][0], 2))
    parts["sw_sinks"] = np.tile(v["sw_sinks"][0][None], (P, 1))
    for n in ("pre_mix_norm", "conv_w", "conv_b", "b_rg", "b_ig", "lru_lambda", "post_mix_norm",
              "pre_ffn_norm", "post_ffn_norm"):
        parts[f"{n}_2"] = columns(v[f"{n}_2"][0])
    return parts


PARAM_WIDTHS = (
    [("c", KT), ("norm_g", 12 * KT), ("ada_b", 36 * KT)]
    + [(f"{n}{j}", w) for j in range(2) for n, w in
       (("rw_mu", 48), ("rw_w0", 8), ("rw_a0", 8), ("rw_k_k", 8), ("rw_k_a", 8), ("rw_r_k", 8),
        ("rw_ln_w", 8), ("rw_ln_b", 8))]
    + [("rw_v0", 8), ("mb_conv_w", 128), ("mb_conv_b", 32), ("mb_dt_bias", 1), ("mb_A_log", 1),
       ("mb_D", 16), ("mb_norm_g", 16), ("sw_q_norm", 1), ("sw_k_norm", 1), ("sw_sinks", 16)]
    + [(f"{n}_2", w) for n, w in
       (("pre_mix_norm", 8), ("conv_w", 32), ("conv_b", 8), ("b_rg", 8), ("b_ig", 8),
        ("lru_lambda", 8), ("post_mix_norm", 8), ("pre_ffn_norm", 8), ("post_ffn_norm", 8))])
PARAM_AT = {}
for _n, _w in PARAM_WIDTHS:
    PARAM_AT[_n] = (sum(w for _, w in PARAM_AT.values()), _w)
PARAMS = sum(w for _, w in PARAM_AT.values())


def const_parts():
    i = np.arange(P)
    row, col = i[:, None], i[None, :]
    same = (row // 64) == (col // 64)
    r, c = row % 64, col % 64
    parts = {
        "ident": row == col,
        "ones": np.ones((P, P)),
        "head_ones": same,
        "stacked_ident": r[:, :] == np.arange(64)[None, :],
        "wkv_mask": np.concatenate([same & (r < c), same & (r <= c)], 1),
    }
    for b in range(6):
        s = 1 << b
        low = same & (r // (2 * s) == c // (2 * s)) & (r // s % 2 == 1) & (c // s % 2 == 0)
        parts[f"level{b}"] = -1.0 * low
    parts["level0_t"] = parts["level0"].T
    pick = np.zeros((P, 47))
    pick[:, 23] = 1
    parts["pick"] = pick
    parts["chunk_reset"] = np.tile(np.arange(T) % 64 != 0, (P, 1))
    parts["ssd_reset"] = np.tile(np.arange(T) % 128 != 0, (P, 1))
    parts["ssd_open"] = np.where(row <= col, 0.0, -1e30)
    parts["ssd_mask"] = row <= col
    t, s = P + row, np.arange(T)[None, :]
    band = np.where((t - s >= 0) & (t - s < 128), 0.0, -1e30)
    parts["sw_band"] = np.concatenate([band[:, P:], band], 1)
    bands = [np.where((t - s >= 0) & ((t - s) % d == 0) & (t - s <= 128 * d), 0.0, -1e30) for d in (1, 4, 16)]
    parts["bands"] = np.concatenate(bands, 1)
    parts["bands_first"] = np.concatenate([b[:, P:] for b in bands], 1)
    for j in range(2):
        parts[f"twice{j}"] = row == j * 64 + c
    rot = np.zeros((P, P))
    rot[np.arange(16) + 16, np.arange(16)] = -1
    rot[np.arange(16), np.arange(16) + 16] = 1
    parts["rotate"] = rot
    freq = np.zeros((P, 1))
    freq[:32, 0] = np.tile(np.float32(500000.0) ** (-np.arange(0, 32, 2, dtype=np.float32) / np.float32(32)), 2)
    parts["inv_freq"] = freq
    parts["eps"] = np.full((P, 1), EPS)
    parts["gn_eps"] = np.full((P, 1), 64e-5)
    return {n: np.ascontiguousarray(a, np.float32) for n, a in parts.items()}


CONST_PARTS = const_parts()
CONST_AT = {}
for _n, _a in CONST_PARTS.items():
    CONST_AT[_n] = (sum(w for _, w in CONST_AT.values()), _a.shape[1])
CONSTS = sum(w for _, w in CONST_AT.values())



class Chip:

    def __init__(self, nc):
        self.nc = nc
        self.sem = {}

    def const(self, name, rows=P):
        at, width = CONST_AT[name]
        return self.consts[0:rows, at:at + width]

    def param(self, name, col=0, n=1, rows=P):
        at, width = PARAM_AT[name]
        assert col + n <= width
        return self.params[0:rows, at + col:at + col + n]

    def tile(self, at, n=KT, width=T):
        a = int(at * 1024)
        return self.arena[:, a:a + n * width].rearrange("p (n t) -> p n t", n=n)


class Products:

    def __init__(self, k, pe):
        self.k, self.pe, self.block, self.freed, self.owed, self.q = k, pe, 0, True, False, 0

    @property
    def slot(self):
        return self.block // BLOCKS

    def take(self, n=1):
        slot, at = divmod(self.block, BLOCKS)
        if at == 0:
            self.pe.wait_ge(self.k.weights_loaded[slot % RING], 16 * (slot // RING + 1))
            self.owed = self.owed or not self.freed
        self.freed = False
        self.block += n
        assert at + n <= BLOCKS
        return self.k.weights[:, slot % RING, at * P:(at + n) * P]

    def mm(self, out, w, x, start, stop, signal=None, turn=None):
        if self.owed and signal is not None:
            self.pe.drain().then_inc(self.k.sem["weights_used"], 1)
            self.owed = False
        ins = self.k.nc.tensor.matmul(out, lhsT=w, rhs=x, start=start, stop=stop, is_transpose=turn)
        if self.owed:
            ins.then_inc(self.k.sem["weights_used"], 1)
            self.owed = False
        elif signal is not None:
            ins.then_inc(signal, 1)

    def turn(self, out, src, signal=None):
        self.mm(out, src, self.k.const("ident"), True, True, signal, turn=True)

    def align(self):
        self.block += -self.block % BLOCKS
        self.owed = not self.freed
        self.freed = True


class Own:

    def __init__(self, eng, sem, base=0):
        self.eng, self.sem, self.base, self.n = eng, sem, base, 0

    def mark(self, ins):
        self.n += 1
        ins.then_inc(self.sem, 1)

    def wait(self):
        self.eng.wait_ge(self.sem, self.base + self.n)

    def of(self, ins):
        self.mark(ins)
        self.wait()


def layout(k, ctx):
    nc = k.nc

    def sb(name, shape, dt=FP32):
        return ctx.enter_context(nc.sbuf_tensor(name, shape, dt))

    k.weights = sb("weights", [P, RING, BLOCKS * P])
    k.ada_in = sb("ada_in", [P, 2, KT, ADA_CHUNK])
    k.ada_sum = sb("ada_sum", [P, ADA_COLS])
    k.x = sb("x", [P, KT, T])
    k.consts = sb("consts", [P, CONSTS])
    k.params = sb("params", [P, PARAMS])
    k.c_act = sb("c_act", [P, KT])
    k.mod = sb("mod", [P, 2, 24])
    k.mod_rows = sb("mod_rows", [24, P])
    k.gain = sb("gain", [P, 2, KT])
    k.half_gate = sb("half_gate", [P, 2, KT])
    k.rms = sb("rms", [P, T])
    k.rstd = sb("rstd", [P, T])
    with ExitStack() as upper:
        def part(name, shape):
            return upper.enter_context(nc.sbuf_tensor(name, shape, FP32R))

        upper.enter_context(nc.sbuf_tensor("arena_lower", [P, 6 * 1024], FP32))
        k.h_part = [part(f"h_part{i}", [P, KT, T]) for i in range(2)]
        k.hidden_part = [part(f"hidden_part{i}", [P, RING, T]) for i in range(2)]
        k.up_part = [part(f"up_part{i}", [P, 2, 2 * KT * P]) for i in range(2)]
        k.down_part = [part(f"down_part{i}", [P, 2, KT * P]) for i in range(2)]
    with ExitStack() as upper:
        upper.enter_context(nc.sbuf_tensor("arena_below_parts", [P, 15 * 1024], FP32))
        k.in_part = [upper.enter_context(nc.sbuf_tensor(f"in_part{i}", [P, KT, T], FP32R)) for i in range(2)]
        k.w_part = [upper.enter_context(nc.sbuf_tensor(f"w_part{i}", [P, RING, KT * P], FP32R)) for i in range(2)]
    k.arena = sb("arena", [P, 27 * 1024])
    k.c_pick = k.ada_sum[:, 0:47 * KT].rearrange("p (t m) -> p t m", t=KT)
    k.small = sb("small", [P, 512])
    k.rope = k.ada_sum[0:32, 0:4 * T].rearrange("p (n t) -> p n t", n=4)
    k.rot_tmp = k.ada_sum[0:32, 4 * T:6 * T].rearrange("p (n t) -> p n t", n=2)
    k.psum = ctx.enter_context(nc.psum_tensor("psum", [P, 8, 512], FP32))
    k.acc = k.psum[:, 4:8, :].rearrange("p b (h t) -> p (b h) t", h=2)
    k.h = k.tile(0)
    k.sq = k.tile(2)
    k.silu = k.tile(4, RING)
    k.hidden = k.tile(5, RING)
    k.weights_loaded = [ctx.enter_context(nc.semaphore(f"weights_loaded{r}")) for r in range(RING)]
    k.ada_loaded = [ctx.enter_context(nc.semaphore(f"ada_loaded{r}")) for r in range(2)]
    for n in ("weights_used", "inputs_loaded", "c_ready", "pool_own", "ada_free", "ada_ready", "mod_summed",
              "mod_rows", "mod_rows_read", "c_silu",
              "mod_ready", "dve_own", "act_own", "x_ready", "squares", "mean_square", "rms_ready",
              "scaled", "h_ready", "gate_up", "silu_ready", "hidden_ready", "out_ready",
              "h_high", "up_high", "up_ready", "down_high", "down_done", "hidden_full", "hidden_high", "stored",
              "projected", "evacuated", "mixed", "conv_opened", "w_high", "w_parted", "in_high", "in_parted",
              "rw_mixed", "rw_kk", "rw_squares", "rw_bonus_in", "rw_head_sum", "rw_norm_read", "rw_norm",
              "rw_cum", "rw_exp", "rw_gated", "v_first_moved", "wkv_free", "wkv_state",
              "wkv_built_upper", "wkv_built_lower", "wkv_outer", "wkv_masked", "wkv_turned",
              "wkv_turned_read", "inv_ready", "inv_lx", "inv_t", "inv_xlx", "wkv_u", "wkv_u_read", "wkv_sa",
              "wkv_sa_read", "wkv_y", "wkv_yt", "wkv_own", "gn_var", "gn_sd", "gn_ready",
              "mb_silu", "mb_a", "mb_dt_abs", "mb_dt_exp", "mb_acum", "mb_cols", "mb_cols_read", "mb_x_turned",
              "mb_x_read", "mb_b_turned", "mb_b_read", "mb_cb", "mb_masked", "mb_seg_sum", "mb_seg", "mb_exp",
              "mb_mt", "mb_y", "mb_y_read", "mb_state_read", "mb_gated", "mb_squares", "mb_group_sum",
              "mb_rms", "mb_normed",
              "at_scored", "at_added", "at_max", "at_exp", "at_prob", "at_turned", "at_turned_read",
              "at_values", "at_out_read", "sw_squares", "sw_head_sum", "sw_rms", "sw_k_normed", "sw_q_normed",
              "sw_k_twice", "sw_k_twice_read",
              "b2_rotated", "b2_rotated_read", "b2_rope", "b2_convolved", "b2_lam_exp", "b2_lam", "b2_angle",
              "b2_sin", "b2_tanh", "b2_decay", "b2_power", "b2_root", "b2_lru", "b2_mixed", "normed", "positions_loaded"):
        k.sem[n] = ctx.enter_context(nc.semaphore(n))



def stream_weights(k, sp, w, slots):
    for n in range(RING):
        sp.dma_start(k.weights[:, n], w[n]).then_inc(k.weights_loaded[n], 16)
    with sp.Fori(1, slots // RING) as g:
        for r in range(RING):
            sp.wait_ge(k.sem["weights_used"], g * RING + (r - RING + 1))
            sp.dma_start(k.weights[:, r], w[g * RING + r]).then_inc(k.weights_loaded[r], 16)



def ada_sums(k, pool, ada_w, units):
    sem, nc = k.sem, k.nc
    own, pairs, halvings = sem["pool_own"], ADA_STEPS // 2, 3
    pool.wait_ge(sem["c_ready"], 1)
    c = k.c_act[:, :].unsqueeze(2).to_broadcast([P, KT, ADA_CHUNK])
    for b in range(2):
        pool.dma_start(k.ada_in[:, b], ada_w[b]).then_inc(k.ada_loaded[b], 16)
    with pool.Fori(0, units) as u:
        with pool.Fori(0, pairs) as i:
            pool.wait_ge(sem["mod_summed"], u + 1)
            for b in range(2):
                buf = k.ada_in[:, b]
                n = u * pairs + i
                done = n * (2 * (1 + halvings)) + b * (1 + halvings)
                pool.wait_ge(k.ada_loaded[b], n * 16 + 16)
                nc.gpsimd.tensor_tensor(buf, buf, c, ALU.mult).then_inc(own, 1)
                for h, rows in enumerate((4, 2, 1)):
                    out = buf[:, 0:rows] if rows > 1 else \
                        k.ada_sum[:, bass.ds(i * (2 * ADA_CHUNK) + b * ADA_CHUNK, ADA_CHUNK)]
                    lo, hi = (buf[:, 0:rows], buf[:, rows:2 * rows]) if rows > 1 else (buf[:, 0], buf[:, 1])
                    pool.wait_ge(own, done + h + 1)
                    nc.gpsimd.tensor_tensor(out, lo, hi, ALU.add).then_inc(own, 1)
                pool.wait_ge(own, done + 1 + halvings)
                pool.dma_start(buf, ada_w[n * 2 + (2 + b)]).then_inc(k.ada_loaded[b], 16)
        pool.drain().then_inc(sem["ada_ready"], 1)
    for b in range(2):
        pool.wait_ge(k.ada_loaded[b], 16 * (units * pairs + 1))


def first_mod_products(k, pe, pr):
    pe.wait_ge(k.sem["c_ready"], 1)
    for m in range(24):
        for t in range(KT):
            pr.mm(k.psum[0:24, 3, 256:384], k.c_pick[:, t, 23 - m:47 - m], pr.take(), (m, t) == (0, 0),
                  (m, t) == (23, KT - 1), k.sem["mod_rows"] if (m, t) == (23, KT - 1) else None)
    turn_mod_rows(k, pe, pr, 0)


def turn_mod_rows(k, pe, pr, u):
    pe.wait_ge(k.sem["mod_rows_read"], u + 1)
    pr.mm(k.psum[:, 3, 256:280], k.mod_rows[:, :], k.const("ident", 24)[:, 0:24], True, True, k.sem["mod_summed"])


def mod_products(k, pe, pr, u):
    pe.wait_ge(k.sem["ada_ready"], u)
    pe.wait_ge(k.sem["mod_ready"], u)
    for m in range(24):
        pr.mm(k.psum[0:24, 3, 256:384], k.const("pick")[:, 23 - m:47 - m], k.ada_sum[:, m * P:(m + 1) * P],
              m == 0, m == 23, k.sem["mod_rows"] if m == 23 else None)
    turn_mod_rows(k, pe, pr, u)


def mod_vector(k, dve, own, u):
    b = u % 2
    dve.wait_ge(k.sem["mod_rows"], u + 1)
    k.nc.vector.tensor_copy(k.mod_rows[:, :], k.psum[0:24, 3, 256:384]).then_inc(k.sem["mod_rows_read"], 1)
    dve.wait_ge(k.sem["mod_summed"], u + 1)
    own.of(k.nc.vector.tensor_tensor(k.mod[:, b, :], k.psum[:, 3, 256:280], k.param("ada_b", 24 * u, 24), ALU.add))
    own.of(k.nc.vector.scalar_tensor_tensor(k.gain[:, b, :], k.mod[:, b, 8:16], 1.0, k.param("norm_g", 8 * u, 8),
                                            ALU.add, ALU.mult))
    k.nc.vector.tensor_scalar(k.half_gate[:, b, :], k.mod[:, b, 16:24], 0.5, None, ALU.mult)\
        .then_inc(k.sem["mod_ready"], 1)



def norm_root(k, act, n):
    act.wait_ge(k.sem["mean_square"], n + 1)
    k.nc.scalar.activation(k.rms[:, :], k.psum[:, 3, 0:T], ACT.Sqrt, bias=k.const("eps"), scale=1.0 / D)\
        .then_inc(k.sem["rms_ready"], 1)


def norm_act(k, act, n, shift=None, ffn=None, parts=None):
    sem = k.sem
    for t in range(KT):
        if n:
            act.wait_ge(sem["x_ready"], KT * ((n if n < 14 else 13) - 1) + t + 1)
        k.nc.scalar.activation(k.sq[:, t], k.x[:, t], ACT.Square).then_inc(sem["squares"], 1)
    if ffn is not None:
        up_high(k, act, ffn, 0, 0)
    if parts is not None:
        for m in range(RING):
            parts.high(act, m)
    norm_root(k, act, n)
    if ffn is not None:
        for t in range(KT):
            act.wait_ge(sem["scaled"], KT * min(n, NORMS) + t + 1)
            if shift is None:
                ins = k.nc.scalar.activation(k.h_part[0][:, t], k.h[:, t], ACT.Copy)
            else:
                ins = k.nc.scalar.activation(k.h_part[0][:, t], k.h[:, t], ACT.Identity, bias=shift[:, t:t + 1])
            ins.then_inc(sem["h_high"], 1)
        return
    if parts is not None:
        for t in range(KT):
            if shift is None:
                act.wait_ge(sem["h_ready"], KT * n + t + 1)
                ins = k.nc.scalar.activation(k.in_part[0][:, t], k.h[:, t], ACT.Copy)
            else:
                act.wait_ge(sem["scaled"], KT * n + t + 1)
                ins = k.nc.scalar.activation(k.in_part[0][:, t], k.h[:, t], ACT.Identity, bias=shift[:, t:t + 1])
            ins.then_inc(sem["in_high"], 1)
    if shift is None:
        return
    for t in range(KT):
        act.wait_ge(sem["scaled"], KT * n + t + 1)
        if parts is not None:
            act.wait_ge(sem["in_parted"], KT * parts.i + t + 1)
        k.nc.scalar.activation(k.h[:, t], k.h[:, t], ACT.Identity, bias=shift[:, t:t + 1])\
            .then_inc(sem["h_ready"], 1)


def norm_products(k, pe, pr, n):
    if n < NORMS:
        pe.wait_ge(k.sem["mod_ready"], n + 1)
    for t in range(KT):
        pe.wait_ge(k.sem["squares"], KT * n + t + 1)
        pr.mm(k.psum[:, 3, 0:T], k.const("ones"), k.sq[:, t], t == 0, t == KT - 1,
              k.sem["mean_square"] if t == KT - 1 else None)


def norm_vector(k, dve, own, n, gain, src=None, signal="scaled", ffn=None, shift=None, parts=None):
    src = k.x if src is None else src
    if ffn is not None:
        up_low(k, dve, ffn, 0, 0)
    if parts is not None:
        for m in range(RING):
            parts.low(dve, m)
    dve.wait_ge(k.sem["rms_ready"], n + 1)
    if n < NORMS:
        dve.wait_ge(k.sem["mod_ready"], n + 1)
    own.of(k.nc.vector.reciprocal(k.rstd[:, :], k.rms[:, :]))
    for t in range(KT):
        k.nc.vector.scalar_tensor_tensor(k.h[:, t], src[:, t], gain[:, t:t + 1], k.rstd[:, :], ALU.mult, ALU.mult)\
            .then_inc(k.sem[signal], 1)
    if ffn is not None:
        for t in range(KT):
            dve.wait_ge(k.sem["h_high"], KT * ffn + t + 1)
            high = k.h_part[0][:, t].bitcast(FP32)
            k.nc.vector.scalar_tensor_tensor(k.h_part[1][:, t], k.h[:, t], 0.0 if shift is None else shift[:, t:t + 1],
                                             high, ALU.add, ALU.subtract).then_inc(k.sem["h_ready"], 1)
    if parts is not None:
        for t in range(KT):
            dve.wait_ge(k.sem["in_high"], KT * parts.i + t + 1)
            high = k.in_part[0][:, t].bitcast(FP32)
            k.nc.vector.scalar_tensor_tensor(k.in_part[1][:, t], k.h[:, t], 0.0 if shift is None else shift[:, t:t + 1],
                                             high, ALU.add, ALU.subtract).then_inc(k.sem["in_parted"], 1)


def residual(k, dve, u, gate, done):
    for t in range(KT):
        done(t)
        k.nc.vector.scalar_tensor_tensor(k.x[:, t], k.acc[:, t], gate[:, t:t + 1], k.x[:, t], ALU.mult, ALU.add)\
            .then_inc(k.sem["x_ready"], 1)



PAIRS = ((0, 0), (0, 1), (1, 0))


def up_high(k, act, i, j, it):
    n = ffn_slot(i) + j
    act.wait_ge(k.weights_loaded[n % RING], it * (FFN_UNROLL // RING * 16) + 16 * (n // RING + 1))
    if j >= 2:
        act.wait_ge(k.sem["gate_up"], it * FFN_UNROLL + (FT * i + j - 1))
    k.nc.scalar.activation(k.up_part[0][:, j % 2], k.weights[:, n % RING, 0:2 * KT * P], ACT.Copy)\
        .then_inc(k.sem["up_high"], 1)


def up_low(k, dve, i, j, it):
    n = ffn_slot(i) + j
    dve.wait_ge(k.sem["up_high"], it * FFN_UNROLL + (FT * i + j + 1))
    if j >= 2:
        dve.wait_ge(k.sem["gate_up"], it * FFN_UNROLL + (FT * i + j - 1))
    k.nc.vector.tensor_tensor(k.up_part[1][:, j % 2], k.weights[:, n % RING, 0:2 * KT * P],
                              k.up_part[0][:, j % 2].bitcast(FP32), ALU.subtract).then_inc(k.sem["up_ready"], 1)


def ffn_products(k, pe, pr, i, tail=lambda: None):
    sem, n0, base, mm = k.sem, pr.slot, FT * i, k.nc.tensor.matmul
    assert n0 == ffn_slot(i)

    def up(j, it):
        pe.wait_ge(sem["up_ready"], it * FFN_UNROLL + (base + j + 1))
        if j >= RING:
            pe.wait_ge(sem["hidden_ready"], it * FFN_UNROLL + (base + j - RING + 1))
        for half in range(2):
            for t in range(KT):
                if j == 0 and half == 0:
                    pe.wait_ge(sem["h_ready"], k.h_at + t + 1)
                b = (half * KT + t) * P
                for n, (wp, xp) in enumerate(PAIRS):
                    ins = mm(k.psum[:, j % RING, half * T:(half + 1) * T], lhsT=k.up_part[wp][:, j % 2, b:b + P],
                             rhs=k.h_part[xp][:, t], start=t == 0 and n == 0, stop=t == KT - 1 and n == 2)
        ins.then_inc(sem["gate_up"], 1)

    def down(j, it, start=False, stop=False):
        pe.wait_ge(sem["hidden_ready"], it * FFN_UNROLL + (base + j + 1))
        pe.wait_ge(sem["weights_used"], it * FFN_UNROLL + (n0 + j + 1))
        for d in range(KT):
            for n, (wp, xp) in enumerate(PAIRS):
                ins = mm(k.acc[:, d], lhsT=k.down_part[wp][:, j % 2, d * P:(d + 1) * P],
                         rhs=k.hidden_part[xp][:, j % RING], start=start and d % 2 == 0 and n == 0,
                         stop=stop and n == 2, skip_group_check=True)
            if d == KT - 1:
                ins.then_inc(sem["down_done"], 1)
            elif stop and d % 2:
                ins.then_inc(sem["out_ready"], 1)

    def step(j, it):
        up(j, it)
        if j:
            down(j - 1, it, start=j == 1)

    ffn_steps(pe, step)
    tail()
    down(FT - 1, 0, stop=True)
    pr.block += FT * BLOCKS
    assert pr.freed and not pr.owed


def ffn_steps(eng, step):
    for j in range(FFN_PEELED):
        step(j, 0)
    with eng.Fori(0, (FT - 1 - FFN_PEELED) // FFN_UNROLL) as it:
        for r in range(FFN_UNROLL):
            step(FFN_PEELED + r, it)
    step(FT - 1, 0)


def ffn_act(k, act, i):
    base, n0, copy = FT * i, ffn_slot(i), ACT.Copy

    def step(j, it):
        if j + 1 < FT:
            up_high(k, act, i, j + 1, it)
        act.wait_ge(k.weights_loaded[(n0 + j) % RING], it * (FFN_UNROLL // RING * 16) + 16 * ((n0 + j) // RING + 1))
        if j >= 2:
            act.wait_ge(k.sem["down_done"], it * FFN_UNROLL + (base + j - 1))
        k.nc.scalar.activation(k.down_part[0][:, j % 2], k.weights[:, (n0 + j) % RING, 2 * KT * P:], copy)\
            .then_inc(k.sem["down_high"], 1)
        act.wait_ge(k.sem["gate_up"], it * FFN_UNROLL + (base + j + 1))
        if j >= RING:
            act.wait_ge(k.sem["hidden_ready"], it * FFN_UNROLL + (base + j - RING + 1))
        k.nc.scalar.activation(k.silu[:, j % RING], k.psum[:, j % RING, 0:T], ACT.Silu)\
            .then_inc(k.sem["silu_ready"], 1)
        act.wait_ge(k.sem["hidden_full"], it * FFN_UNROLL + (base + j + 1))
        if j >= RING:
            act.wait_ge(k.sem["down_done"], it * FFN_UNROLL + (base + j - RING + 1))
        k.nc.scalar.activation(k.hidden_part[0][:, j % RING], k.hidden[:, j % RING], copy)\
            .then_inc(k.sem["hidden_high"], 1)

    ffn_steps(act, step)


def ffn_vector(k, dve, i):
    base, n0, v, sub = FT * i, ffn_slot(i), k.nc.vector, ALU.subtract

    def step(j, it):
        if j + 1 < FT:
            up_low(k, dve, i, j + 1, it)
        dve.wait_ge(k.sem["down_high"], it * FFN_UNROLL + (base + j + 1))
        v.tensor_tensor(k.down_part[1][:, j % 2], k.weights[:, (n0 + j) % RING, 2 * KT * P:],
                        k.down_part[0][:, j % 2].bitcast(FP32), sub).then_inc(k.sem["weights_used"], 1)
        dve.wait_ge(k.sem["silu_ready"], it * FFN_UNROLL + (base + j + 1))
        if j >= RING:
            dve.wait_ge(k.sem["hidden_ready"], it * FFN_UNROLL + (base + j - RING + 1))
        v.tensor_tensor(k.hidden[:, j % RING], k.silu[:, j % RING], k.psum[:, j % RING, T:2 * T], ALU.mult)\
            .then_inc(k.sem["hidden_full"], 1)
        dve.wait_ge(k.sem["hidden_high"], it * FFN_UNROLL + (base + j + 1))
        v.tensor_tensor(k.hidden_part[1][:, j % RING], k.hidden[:, j % RING],
                        k.hidden_part[0][:, j % RING].bitcast(FP32), sub).then_inc(k.sem["hidden_ready"], 1)

    ffn_steps(dve, step)


def ffn_residual_wait(k, dve, i):
    def done(t):
        if t < KT - 2:
            dve.wait_ge(k.sem["out_ready"], (KT // 2 - 1) * i + t // 2 + 1)
        else:
            dve.wait_ge(k.sem["down_done"], FT * (i + 1))
    return done



def project(k, pe, pr, x, kt, m=P, rows=P, before=None):
    bank = pr.q % RING
    if pr.q >= RING:
        pe.wait_ge(k.sem["evacuated"], pr.q - RING + 1)
    for t in range(kt):
        if before is not None:
            before(t)
        w = pr.take()
        pr.mm(k.psum[0:m, bank, 0:T], w[0:rows, 0:m], x(t), t == 0, t == kt - 1,
              k.sem["projected"] if t == kt - 1 else None)
    pr.q += 1


class Parts:

    COUNTS = (48, 10, 40)

    def __init__(self, k, i, slot, q0):
        self.k, self.i, self.slot, self.q0 = k, i, slot, q0
        self.tiles, self.before = self.COUNTS[i], sum(self.COUNTS[:i])

    def weights(self, m):
        slot, at = divmod(self.slot * BLOCKS + KT * m, BLOCKS)
        return slot, self.k.weights[:, slot % RING, at * P:(at + KT) * P]

    def high(self, act, m):
        if m >= self.tiles:
            return
        slot, w = self.weights(m)
        act.wait_ge(self.k.weights_loaded[slot % RING], 16 * (slot // RING + 1))
        if m >= RING:
            act.wait_ge(self.k.sem["projected"], self.q0 + m - RING + 1)
        self.k.nc.scalar.activation(self.k.w_part[0][:, m % RING], w, ACT.Copy).then_inc(self.k.sem["w_high"], 1)

    def low(self, dve, m):
        if m >= self.tiles:
            return
        dve.wait_ge(self.k.sem["w_high"], self.before + m + 1)
        self.k.nc.vector.tensor_tensor(self.k.w_part[1][:, m % RING], self.weights(m)[1],
                                       self.k.w_part[0][:, m % RING].bitcast(FP32), ALU.subtract)\
            .then_inc(self.k.sem["w_parted"], 1)

    def products(self, pe, pr):
        k = self.k
        for m in range(self.tiles):
            bank = pr.q % RING
            pe.wait_ge(k.sem["evacuated"], pr.q - RING + 1)
            pe.wait_ge(k.sem["w_parted"], self.before + m + 1)
            for t in range(KT):
                if m == 0:
                    pe.wait_ge(k.sem["in_parted"], KT * self.i + t + 1)
                pr.take()
                for n, (wp, xp) in enumerate(PAIRS):
                    pr.mm(k.psum[:, bank, 0:T], k.w_part[wp][:, m % RING, t * P:(t + 1) * P], k.in_part[xp][:, t],
                          t == 0 and n == 0, t == KT - 1 and n == 2,
                          k.sem["projected"] if t == KT - 1 and n == 2 else None)
            pr.q += 1


class Evacuation:

    def __init__(self, k, act):
        self.k, self.act, self.q = k, act, 0

    def tile(self, out, func, m=P, bias=None, scale=1.0, width=T):
        k, bank = self.k, self.q % RING
        self.act.wait_ge(k.sem["projected"], self.q + 1)
        kw = {} if bias is None else {"bias": bias}
        k.nc.scalar.activation(out, k.psum[0:m, bank, 0:width], func, scale=scale, **kw)\
            .then_inc(k.sem["evacuated"], 1)
        self.q += 1


def output_products(k, pe, pr, kt, x, before):
    for d in range(KT):
        for t in range(kt):
            if d == 0:
                before(t)
            pr.mm(k.acc[:, d], pr.take(), x(t), t == 0, t == kt - 1,
                  k.sem["mixed"] if t == kt - 1 and d % 2 else None)
    pr.align()


def mixed_wait(k, dve, m):
    return lambda t: dve.wait_ge(k.sem["mixed"], KT // 2 * m + t // 2 + 1)



DECAY = float(np.exp(np.float32(-0.5)))
CHUNK = 64
CHUNKS = T // CHUNK
LEVELS = 6
RW_MIXES = (2, 1, 4, 0, 3, 5)
WKV_DVE = 26


def rw_tiles(j):
    names = [("k", 8), ("w1", 1), ("a1", 1), ("w2", 8), ("a2", 8), ("r", 8), ("v", 8)] + [("v1", 1)] * j + \
        [("g1", 2)] + [("v2", 8)] * j + [("g2", 8)]
    at, out = 0, {}
    for n, c in names:
        out[n] = (at, c)
        at += c
    out["end"] = (at, 0)
    return out


class RwTiles:

    def __init__(self, k):
        self.h, self.dx = k.tile(0), k.tile(2)
        self.mix = [k.tile(4), k.tile(6)]
        self.lora = k.tile(8, 5)
        self.sg = k.tile(10)
        self.r, self.k, self.a, self.v, self.g = (k.tile(u) for u in (12, 14, 16, 18, 20))
        self.bv, self.kk = k.tile(22), k.tile(24)
        self.cum, self.v_first, self.e_out, self.e_in = (k.tile(u) for u in (0, 2, 4, 6))
        self.tmp, self.norm = self.g, self.bv
        self.one_less_ka = k.small[:, 0:8]
        self.p_end = k.small[:, 8:40].rearrange("p (c n) -> p c n", c=CHUNKS)
        self.stat = [k.small[:, 40 + 16 * i:56 + 16 * i] for i in range(2)]
        self.kr, self.x, self.y, self.am, self.t = [], [], [], [], []
        self.bi_t, self.ki_t, self.vt, self.u, self.sa = [], [], [], [], []
        for hf in range(2):
            at = [hf * 6144]

            def cut(n, *dims):
                a = k.arena[:, at[0]:at[0] + n]
                at[0] += n
                return a
            self.kr.append(cut(1024).rearrange("p (n b c) -> p n b c", n=4, b=2))
            self.x.append(cut(512).rearrange("p (n c) -> p n c", n=4))
            self.y.append(cut(512).rearrange("p (n c) -> p n c", n=4))
            self.am.append(cut(2048).rearrange("p (a n b c) -> p a n b c", a=2, n=4, b=2))
            self.t.append(cut(512).rearrange("p (n c) -> p n c", n=4))
            self.bi_t.append(cut(512).rearrange("p (n c) -> p n c", n=4))
            self.ki_t.append(cut(512).rearrange("p (n c) -> p n c", n=4))
            self.vt.append(cut(256).rearrange("p (n c) -> p n c", n=4))
            self.u.append(cut(256).rearrange("p (n c) -> p n c", n=4))
            last = k.arena[:, 26 * 1024 + hf * 256:26 * 1024 + (hf + 1) * 256]
            self.sa.append(last.rearrange("p (n c) -> p n c", n=4))
        self.state = k.arena[:, 26 * 1024 + 512:27 * 1024].rearrange("p (n c) -> p n c", n=8)


def rw_products(k, pe, pr, j, n, tail):
    s, z, tiles = k.sem, RwTiles(k), rw_tiles(j)
    mm = pr.mm
    mixes = iter(range(6))

    def mixed():
        i = next(mixes)
        at = 48 * j + KT * i
        return dict(x=lambda t: z.mix[i % 2][:, t], kt=KT), lambda t: pe.wait_ge(s["rw_mixed"], at + t + 1)

    q0 = pr.q

    def evacuated(name):
        pe.wait_ge(s["evacuated"], q0 + tiles[name][0] + tiles[name][1])

    def full():
        kw, before = mixed()
        for m in range(KT):
            project(k, pe, pr, before=before if m == 0 else None, **kw)
        return kw

    def expand(src, at, rows):
        evacuated(src)
        for m in range(KT):
            project(k, pe, pr, x=lambda t: z.lora[0:rows, at], kt=1, rows=rows)

    def head_sums(i):
        for t in range(KT):
            pe.wait_ge(s[("rw_squares", "rw_bonus_in")[i]], KT * j + t + 1)
            if i and t == 0:
                pe.wait_ge(s["rw_norm_read"], j + 1)
            mm(k.acc[:, t], k.const("head_ones"), (z.norm, z.tmp)[i][:, t], True, True,
               s["rw_head_sum"] if t % 2 else None)

    full()
    for m in (64, 64):
        kw, before = mixed()
        project(k, pe, pr, m=m, before=before, **kw)
    expand("w1", 1, 64)
    expand("a1", 2, 64)
    full()
    head_sums(0)
    kw = full()
    if j:
        project(k, pe, pr, m=32, **kw)
    head_sums(1)
    kw, before = mixed()
    project(k, pe, pr, m=P, before=before, **kw)
    project(k, pe, pr, m=32, **kw)
    if j:
        expand("v1", 0, 32)
    evacuated("g1")
    for m in range(KT):
        bank = pr.q % RING
        pe.wait_ge(s["evacuated"], pr.q - RING + 1)
        mm(k.psum[:, bank, 0:T], pr.take(), z.lora[:, 3], True, False)
        mm(k.psum[:, bank, 0:T], pr.take()[0:32], z.lora[0:32, 4], False, True, s["projected"])
        pr.q += 1

    with pe.Fori(0, CHUNKS) as c:
        def at(name, per, i):
            pe.wait_ge(s[name], c * per + (CHUNKS * per * j + i))

        def bank(hf, b):
            return k.psum[:, 4 * hf + b, :]

        for hf in range(2):
            pe.wait_ge(s["wkv_free"], c * 2 + (10 * j + hf + 1))
            at("wkv_built_upper", 2, hf + 1)
            at("wkv_built_lower", 2, hf + 1)
            for i, src in enumerate((z.x, z.y)):
                for p in range(4):
                    mm(bank(hf, 2 * i + p // 2)[:, p % 2 * 256:p % 2 * 256 + 256], src[hf][:, p],
                       z.kr[hf][:, p].rearrange("p b c -> p (b c)"), True, True,
                       s["wkv_outer"] if i == 1 and p == 3 else None)
        for hf in range(2):
            at("wkv_masked", 2, hf + 1)
            for b, src in ((0, z.y), (1, z.x)):
                for p in range(4):
                    pr.turn(bank(hf, b)[:, p * P:(p + 1) * P], src[hf][:, p])
            for p in range(4):
                mm(bank(hf, 2)[:, p * 64:(p + 1) * 64], z.t[hf][:, p], k.const("stacked_ident"), True, True)
            for p in range(4):
                pr.turn(bank(hf, 3)[:, p * P:(p + 1) * P], z.am[hf][:, 0, p, 0],
                        s["wkv_turned"] if p == 3 else None)
        for lv in range(1, LEVELS):
            for hf in range(2):
                at("inv_ready", 2 * LEVELS, 2 * (lv - 1) + hf + 1)
                for p in range(4):
                    mm(bank(hf, 3)[:, p * P:(p + 1) * P], z.am[hf][:, 0, p, 0], z.x[hf][:, p], True, True,
                       s["inv_lx"] if p == 3 else None)
            for hf in range(2):
                at("inv_t", 2 * (LEVELS - 1), 2 * (lv - 1) + hf + 1)
                if lv == 1:
                    at("wkv_turned_read", 2, hf + 1)
                if lv < LEVELS - 1:
                    for p in range(4):
                        mm(bank(hf, 0)[:, p * P:(p + 1) * P], z.y[hf][:, p], z.t[hf][:, p], True, True)
                for p in range(4):
                    mm(bank(hf, 1)[:, p * P:(p + 1) * P], z.t[hf][:, p], z.y[hf][:, p], True, True,
                       s["inv_xlx"] if p == 3 else None)
        for hf in range(2):
            pe.wait_ge(s["wkv_state"], c * 2 + (10 * j + hf + 1))
            if LEVELS == 1:
                at("wkv_turned_read", 2, hf + 1)
            for p in range(4):
                o = bank(hf, 2)[:, p * 64:(p + 1) * 64]
                mm(o, z.kr[hf][:, p, 0], z.state[:, 4 * hf + p], True, False)
                mm(o, z.am[hf][:, 1, p, 0], z.vt[hf][:, p], False, True, s["wkv_u"] if p == 3 else None)
        for hf in range(2):
            at("wkv_u_read", 2, hf + 1)
            at("inv_ready", 2 * LEVELS, 2 * (LEVELS - 1) + hf + 1)
            for p in range(4):
                mm(bank(hf, 3)[:, p * 64:(p + 1) * 64], z.y[hf][:, p], z.u[hf][:, p], True, True,
                   s["wkv_sa"] if p == 3 else None)
        for hf in range(2):
            at("wkv_sa_read", 2, hf + 1)
            for p in range(4):
                o = bank(hf, 2)[:, p * 64:(p + 1) * 64]
                mm(o, z.kr[hf][:, p, 1], z.state[:, 4 * hf + p], True, False)
                mm(o, z.am[hf][:, 0, p, 1], z.sa[hf][:, p], False, False)
                mm(o, z.am[hf][:, 1, p, 1], z.vt[hf][:, p], False, True)
            for p in range(4):
                o = bank(hf, 0)[:, p * 64:(p + 1) * 64]
                mm(o, z.bi_t[hf][:, p], z.sa[hf][:, p], True, False)
                mm(o, z.ki_t[hf][:, p], z.vt[hf][:, p], False, True, s["wkv_y"] if p == 3 else None)
        for hf in range(2):
            at("gn_ready", 2, hf + 1)
            for p in range(4):
                mm(bank(hf, 1)[:, p * 64:(p + 1) * 64], z.kr[hf][:, p, 0], k.const("stacked_ident"), True, True,
                   s["wkv_yt"] if p == 3 else None)
    tail()
    output_products(k, pe, pr, KT, lambda t: z.r[:, t],
                    lambda t: pe.wait_ge(s["rw_gated"], KT * j + t + 1))


def rw_act(k, act, ev, j, v_first):
    s, z, f = k.sem, RwTiles(k), ACT
    act_ = k.nc.scalar.activation
    q0 = ev.q
    for m in range(KT):
        ev.tile(z.k[:, m], f.Copy)
    ev.tile(z.lora[0:64, 1], f.Tanh, m=64)
    ev.tile(z.lora[0:64, 2], f.Copy, m=64)
    for m in range(KT):
        ev.tile(z.sg[:, m], f.Sigmoid, bias=k.param(f"rw_w0{j}", m))
    for m in range(KT):
        ev.tile(z.a[:, m], f.Sigmoid, bias=k.param(f"rw_a0{j}", m))
    for t in range(KT):
        act.wait_ge(s["rw_kk"], KT * j + t + 1)
        act_(z.norm[:, t], z.kk[:, t], f.Square).then_inc(s["rw_squares"], 1)
    for m in range(KT):
        ev.tile(z.r[:, m], f.Copy)
    for m in range(KT):
        ev.tile(z.v[:, m], f.Copy)
        if m == 1:
            act.wait_ge(s["rw_norm_read"], j + 1)
            act_(z.norm, z.norm, f.Sqrt).then_inc(s["rw_norm"], 1)
    if j == 0:
        act.wait_ge(s["evacuated"], ev.q)
        act.dma_start(v_first, z.v).then_inc(s["v_first_moved"], 16)
    else:
        act.wait_ge(s["v_first_moved"], 16)
        act.wait_ge(s["rw_mixed"], 48 * (j + 1))
        act.dma_start(z.v_first, v_first).then_inc(s["v_first_moved"], 16)
        ev.tile(z.lora[0:32, 0], f.Copy, m=32)
    act.wait_ge(s["rw_cum"], 2 * j + 1)
    act_(z.e_out, z.cum, f.Exp, scale=DECAY).then_inc(s["rw_exp"], 1)
    ev.tile(z.lora[:, 3], f.Sigmoid)
    ev.tile(z.lora[0:32, 4], f.Sigmoid, m=32)
    act_(z.e_in, z.cum, f.Exp, scale=-DECAY).then_inc(s["rw_exp"], 1)
    act.wait_ge(s["rw_cum"], 2 * j + 2)
    act.wait_ge(s["rw_exp"], 3 * j + 2)
    act_(z.cum, z.sg, f.Exp, scale=-DECAY).then_inc(s["rw_exp"], 1)
    if j:
        for m in range(KT):
            ev.tile(z.bv[:, m], f.Sigmoid, bias=k.param("rw_v0", m))
    for m in range(KT):
        ev.tile(z.g[:, m], f.Copy)

    with act.Fori(0, CHUNKS) as c:
        def at(name, per, i):
            act.wait_ge(s[name], c * per + (CHUNKS * per * j + i))

        for hf in range(2):
            act.wait_ge(s["wkv_free"], c * 2 + (10 * j + hf + 1))
            for n, (dst, src) in enumerate(rw_builds(z, hf)):
                ins = act_(dst[64:P, :, 64:P], src[64:P, 4 * hf:4 * hf + 4, bass.ds(c * CHUNK, CHUNK)], f.Copy)
            ins.then_inc(s["wkv_built_lower"], 1)
        for hf in range(2):
            at("wkv_turned", 2, hf + 1)
            act_(z.ki_t[hf], k.psum[:, 4 * hf, :].rearrange("p (n c) -> p n c", n=4), f.Copy)
            act_(z.bi_t[hf], k.psum[:, 4 * hf + 1, :].rearrange("p (n c) -> p n c", n=4), f.Copy)
            act_(z.vt[hf], k.psum[:, 4 * hf + 2, 0:256].rearrange("p (n c) -> p n c", n=4), f.Copy)\
                .then_inc(s["wkv_turned_read"], 1)
        for hf in range(2):
            at("wkv_u", 2, hf + 1)
            act_(z.u[hf], k.psum[:, 4 * hf + 2, 0:256].rearrange("p (n c) -> p n c", n=4), f.Copy, scale=-1.0)\
                .then_inc(s["wkv_u_read"], 1)
        for hf in range(2):
            at("wkv_sa", 2, hf + 1)
            act_(z.sa[hf], k.psum[:, 4 * hf + 3, 0:256].rearrange("p (n c) -> p n c", n=4), f.Copy)\
                .then_inc(s["wkv_sa_read"], 1)
        for hf in range(2):
            at("gn_var", 2, hf + 1)
            act_(z.stat[hf][:, 4:8], z.stat[hf][:, 4:8], f.Sqrt, bias=k.const("gn_eps"), scale=1.0 / 64)\
                .then_inc(s["gn_sd"], 1)
        for hf in range(2):
            at("wkv_yt", 2, hf + 1)
            act_(z.r[:, 4 * hf:4 * hf + 4, bass.ds(c * CHUNK, CHUNK)],
                 k.psum[:, 4 * hf + 1, 0:256].rearrange("p (n c) -> p n c", n=4), f.Copy)\
                .then_inc(s["wkv_free"], 1)


def rw_builds(z, hf):
    return [(z.kr[hf][:, :, 0], z.kk), (z.kr[hf][:, :, 1], z.r), (z.x[hf], z.a), (z.y[hf], z.k), (z.t[hf], z.v)]


def rw_vector(k, dve, own, n, j, q0):
    s, z, v, tiles = k.sem, RwTiles(k), k.nc.vector, rw_tiles(j)
    mult, add, sub = ALU.mult, ALU.add, ALU.subtract

    def evacuated(name, m=None):
        first, count = tiles[name]
        dve.wait_ge(s["evacuated"], q0 + first + (count if m is None else m + 1))

    def projected(name):
        dve.wait_ge(s["projected"], q0 + tiles[name][0] + tiles[name][1])

    dve.wait_ge(s["h_ready"], KT * (n + 1))
    own.mark(v.tensor_tensor(z.dx[:, :, 1:T], z.h[:, :, 0:T - 1], z.h[:, :, 1:T], sub))
    own.of(v.tensor_scalar(z.dx[:, :, 0:1], z.h[:, :, 0:1], -1.0, None, mult))

    def mix(i):
        if i >= 2:
            projected(("k", "w1", "a1", "r")[i - 2])
        for t in range(KT):
            v.scalar_tensor_tensor(z.mix[i % 2][:, t], z.dx[:, t], k.param(f"rw_mu{j}", KT * RW_MIXES[i] + t),
                                   z.h[:, t], mult, add).then_inc(s["rw_mixed"], 1)

    for i in range(5):
        mix(i)
    own.mark(v.tensor_scalar(z.one_less_ka, k.param(f"rw_k_a{j}", 0, KT), -1.0, 1.0, mult, add))
    evacuated("k")
    for t in range(KT):
        v.tensor_scalar(z.kk[:, t], z.k[:, t], k.param(f"rw_k_k{j}", t), None, mult).then_inc(s["rw_kk"], 1)
    evacuated("a2")
    own.wait()
    for t in range(KT):
        own.mark(v.tensor_scalar(z.tmp[:, t], z.a[:, t], k.param(f"rw_k_a{j}", t), z.one_less_ka[:, t:t + 1],
                                 mult, add))
    own.wait()
    dve.wait_ge(s["rw_kk"], KT * (j + 1))
    own.of(v.tensor_tensor(z.k, z.k, z.tmp, mult))
    mix(5)
    dve.wait_ge(s["rw_mixed"], 48 * (j + 1))
    for t in range(KT):
        ins = v.tensor_tensor_scan(z.cum[:, t], k.const("chunk_reset"), z.sg[:, t], 0.0, mult, add)
    ins.then_inc(s["rw_cum"], 1)
    evacuated("r")
    for t in range(KT):
        v.scalar_tensor_tensor(z.tmp[:, t], z.r[:, t], k.param(f"rw_r_k{j}", t), z.k[:, t], mult, mult)\
            .then_inc(s["rw_bonus_in"], 1)
    for b in range(4):
        dve.wait_ge(s["rw_head_sum"], 8 * j + b + 1)
        ins = v.tensor_scalar(z.norm[:, 2 * b:2 * b + 2], k.acc[:, 2 * b:2 * b + 2], 1e-24, None, ALU.max)
    ins.then_inc(s["rw_norm_read"], 1)
    dve.wait_ge(s["rw_norm"], j + 1)
    own.of(v.reciprocal(z.norm, z.norm))
    own.of(v.tensor_tensor(z.kk, z.kk, z.norm, mult))
    own.of(v.tensor_tensor(z.a, z.a, z.kk, mult))
    dve.wait_ge(s["rw_cum"], 2 * j + 1)
    v.tensor_tensor(z.sg, z.cum, z.sg, sub).then_inc(s["rw_cum"], 1)
    dve.wait_ge(s["rw_bonus_in"], KT * (j + 1))
    dve.wait_ge(s["rw_exp"], 3 * j + 1)
    own.mark(v.tensor_tensor(z.k, z.k, z.e_out, mult))
    own.mark(v.tensor_tensor(z.a, z.a, z.e_out, mult))
    dve.wait_ge(s["rw_exp"], 3 * j + 2)
    own.mark(v.tensor_tensor(z.r, z.r, z.e_in, mult))
    own.mark(v.tensor_copy(z.p_end, z.e_in[:, :, CHUNK - 1::CHUNK].rearrange("p n c -> p c n")))
    dve.wait_ge(s["rw_exp"], 3 * j + 3)
    own.of(v.tensor_tensor(z.kk, z.kk, z.cum, mult))
    if j:
        evacuated("v2")
        dve.wait_ge(s["v_first_moved"], 32)
        own.of(v.tensor_tensor(z.v_first, z.v_first, z.v, sub))
        own.of(v.tensor_tensor(z.v_first, z.v_first, z.bv, mult))
        own.of(v.tensor_tensor(z.v, z.v, z.v_first, add))
    evacuated("v")
    for b in range(4):
        dve.wait_ge(s["rw_head_sum"], 8 * j + 4 + b + 1)
        own.mark(v.tensor_tensor(z.bv[:, 2 * b:2 * b + 2], k.acc[:, 2 * b:2 * b + 2], z.v[:, 2 * b:2 * b + 2], mult))
    own.mark(v.memset(z.state, 0.0))
    for hf in range(2):
        if hf:
            projected("end")
        for buf in (z.kr[hf], z.x[hf], z.y[hf]):
            own.mark(v.memset(buf, 0.0))
        own.of(v.memset(z.t[hf], 0.0))
        v.tensor_copy(k.small[:, 100 + hf:101 + hf], k.const("eps")).then_inc(s["wkv_free"], 1)
        v.tensor_copy(k.small[:, 102 + hf:103 + hf], k.const("eps")).then_inc(s["wkv_state"], 1)

    with dve.Fori(0, CHUNKS) as c:
        def at(name, per, i):
            dve.wait_ge(s[name], c * per + (CHUNKS * per * j + i))

        def bank(hf, b, n=4, w=P):
            return k.psum[:, 4 * hf + b, 0:n * w].rearrange("p (n c) -> p n c", n=n)

        step = Own(dve, s["wkv_own"], c * WKV_DVE + CHUNKS * WKV_DVE * j)
        for hf in range(2):
            dve.wait_ge(s["wkv_free"], c * 2 + (10 * j + hf + 1))
            for dst, src in rw_builds(z, hf):
                ins = v.tensor_copy(dst[0:64, :, 0:64], src[0:64, 4 * hf:4 * hf + 4, bass.ds(c * CHUNK, CHUNK)])
            ins.then_inc(s["wkv_built_upper"], 1)
        mask = k.const("wkv_mask").unsqueeze(1).to_broadcast([P, 2, 256])
        for hf in range(2):
            at("wkv_outer", 2, hf + 1)
            for i in range(2):
                for half in range(2):
                    ins = v.tensor_tensor(z.am[hf][:, i, 2 * half:2 * half + 2].rearrange("p n b c -> p n (b c)"),
                                          bank(hf, 2 * i + half, 2, 256), mask, mult)
            ins.then_inc(s["wkv_masked"], 1)

        def each(name):
            return k.const(name).unsqueeze(1).to_broadcast([P, 4, P])

        for hf in range(2):
            at("wkv_turned", 2, hf + 1)
            step.mark(v.tensor_tensor(z.x[hf], bank(hf, 3), each("level0"), mult))
            at("wkv_masked", 2, hf + 1)
            step.of(v.tensor_tensor(z.y[hf], z.am[hf][:, 0, :, 0], each("level0_t"), mult))
            step.mark(v.tensor_tensor(z.x[hf], z.x[hf], each("ident"), add))
            step.wait()
            v.tensor_tensor(z.y[hf], z.y[hf], each("ident"), add).then_inc(s["inv_ready"], 1)
        for lv in range(1, LEVELS):
            for hf in range(2):
                at("inv_lx", 2 * (LEVELS - 1), 2 * (lv - 1) + hf + 1)
                v.tensor_tensor(z.t[hf], bank(hf, 3), each(f"level{lv}"), mult).then_inc(s["inv_t"], 1)
            for hf in range(2):
                at("inv_xlx", 2 * (LEVELS - 1), 2 * (lv - 1) + hf + 1)
                at("inv_ready", 2 * LEVELS, 2 * (lv - 1) + hf + 1)
                if lv < LEVELS - 1:
                    step.mark(v.tensor_tensor(z.x[hf], z.x[hf], bank(hf, 0), add))
                    step.wait()
                v.tensor_tensor(z.y[hf], z.y[hf], bank(hf, 1), add).then_inc(s["inv_ready"], 1)
        for hf in range(2):
            st, x4 = z.stat[hf], slice(4 * hf, 4 * hf + 4)
            y, yc, sq = bank(hf, 2, 4, 64), z.u[hf], z.sa[hf]
            at("wkv_y", 2, hf + 1)
            step.mark(v.tensor_reduce(st[:, 0:4], y, AX.X, add))
            step.of(v.tensor_tensor(z.state[:, x4], z.state[:, x4], bank(hf, 0, 4, 64), add))
            v.tensor_tensor(z.state[:, x4], z.state[:, x4],
                            z.p_end[:, bass.ds(c, 1), x4].rearrange("p c n -> p n c").to_broadcast([P, 4, 64]),
                            mult).then_inc(s["wkv_state"], 1)
            step.of(v.tensor_scalar(st[:, 0:4], st[:, 0:4], 1.0 / 64, None, mult))
            step.of(v.tensor_tensor(yc, y, st[:, 0:4].unsqueeze(2).to_broadcast([P, 4, 64]), sub))
            step.of(v.tensor_tensor(sq, yc, yc, mult))
            v.tensor_reduce(st[:, 4:8], sq, AX.X, add).then_inc(s["gn_var"], 1)
        for hf in range(2):
            st = z.stat[hf]
            at("gn_sd", 2, hf + 1)
            step.of(v.reciprocal(st[:, 8:12], st[:, 4:8]))
            for i in range(2):
                rows = slice(64 * i, 64 * i + 64)
                ins = v.tensor_tensor(z.kr[hf][rows, :, 0, rows], z.u[hf][rows],
                                      st[rows, 8:12].unsqueeze(2).to_broadcast([64, 4, 64]), mult)
            ins.then_inc(s["gn_ready"], 1)
        assert step.n == WKV_DVE, step.n
    for t in range(KT):
        dve.wait_ge(s["wkv_free"], 10 * j + 10)
        own.of(v.tensor_scalar(z.r[:, t], z.r[:, t], k.param(f"rw_ln_w{j}", t), k.param(f"rw_ln_b{j}", t), mult, add))
        own.of(v.tensor_tensor(z.r[:, t], z.r[:, t], z.bv[:, t], add))
        v.tensor_tensor(z.r[:, t], z.r[:, t], z.g[:, t], mult).then_inc(s["rw_gated"], 1)
    if j == 0:
        dve.wait_ge(s["v_first_moved"], 16)


def softplus_vector(k, own, out, x, e, z, z2):
    v = k.nc.vector
    own.of(v.tensor_scalar(z, e, 2.0, None, ALU.add))
    own.of(v.reciprocal(z, z))
    own.of(v.tensor_tensor(z, z, e, ALU.mult))
    own.of(v.tensor_tensor(z2, z, z, ALU.mult))
    own.of(v.tensor_scalar(e, z2, 1.0 / 15, None, ALU.mult))
    for n in (13, 11, 9, 7, 5, 3):
        own.of(v.scalar_tensor_tensor(e, e, 1.0 / n, z2, ALU.add, ALU.mult))
    own.of(v.scalar_tensor_tensor(e, e, 1.0, z, ALU.add, ALU.mult))
    own.of(v.tensor_scalar(z, x, 0.0, None, ALU.max))
    own.of(v.scalar_tensor_tensor(out, e, 2.0, z, ALU.mult, ALU.add))


def conv_act(k, act, q, out, name, m, tiles):
    act.wait_ge(k.sem["projected"], q + 1)
    k.nc.scalar.activation(out, k.psum[:, q % RING, 0:T], ACT.Identity, bias=k.param(name[1], m),
                           scale=k.param(name[0], 3 * tiles + m)).then_inc(k.sem["conv_opened"], 1)


def conv_vector(k, dve, own, q, out, name, m, tiles, n):
    v, ps = k.nc.vector, k.psum[:, q % RING, 0:T]
    dve.wait_ge(k.sem["conv_opened"], n + 1)
    for tap in (2, 1, 0):
        n = 3 - tap
        ins = v.scalar_tensor_tensor(out[:, n:T], ps[:, 0:T - n], k.param(name[0], tap * tiles + m), out[:, n:T],
                                     ALU.mult, ALU.add)
        if tap:
            own.of(ins)
    ins.then_inc(k.sem["evacuated"], 1)



MB_TILES = 49
MB_STEPS = 16


class MbTiles:
    def __init__(self, k):
        self.h, self.z, self.x, self.b, self.c = k.tile(0), k.tile(2, 16), k.tile(6, 16), k.tile(10), k.tile(12)
        self.e = [k.arena[:, (14 + 2 * i) * 1024:(14 + 2 * i) * 1024 + 512].rearrange("p (h l) -> p h l", h=4)
                  for i in range(2)]
        self.mt = [k.arena[:, (14 + 2 * i) * 1024 + 512:(15 + 2 * i) * 1024].rearrange("p (h l) -> p h l", h=4)
                   for i in range(2)]
        self.ce = [k.arena[:, (15 + 2 * i) * 1024:(15 + 2 * i) * 1024 + 512].rearrange("p (h l) -> p h l", h=4)
                   for i in range(2)]
        self.cb = [k.arena[:, (15 + 2 * i) * 1024 + 512:(15 + 2 * i) * 1024 + 640] for i in range(2)]
        self.xd = [k.arena[:, (15 + 2 * i) * 1024 + 640:(15 + 2 * i) * 1024 + 896]
                   .rearrange("p (h d) -> p h d", h=4) for i in range(2)]
        self.rms = [k.tile(14, 4)[:, i] for i in range(4)]
        self.xt = k.arena[:, 18 * 1024:22 * 1024].rearrange("p (b h d) -> p b h d", b=2, h=32)
        self.bt = k.arena[:, 22 * 1024:23 * 1024].rearrange("p (g n) -> p g n", g=8)
        self.state = k.arena[:, 24 * 1024:26 * 1024].rearrange("p (h d) -> p h d", h=32)
        self.sq = k.tile(0)
        rows = k.arena[0:32, 26 * 1024:27 * 1024].rearrange("p (n t) -> p n t", n=4)
        self.acum, self.dt, self.dtx, self.e32 = (rows[:, i] for i in range(4))
        more = k.arena[0:32, 23 * 1024:23 * 1024 + 768].rearrange("p (n t) -> p n t", n=3)
        self.z32, self.z32b, self.da = (more[:, i] for i in range(3))
        self.cols = k.small[:, 128:256].rearrange("p (w b h) -> p w b h", w=2, b=2)
        self.neg_a = k.small[0:32, 104:105]

    def conv(self, m):
        return self.x[:, m] if m < 16 else self.b[:, m - 16] if m < 24 else self.c[:, m - 24]


def mb_products(k, pe, pr, u, tail, parts):
    s, z, mm = k.sem, MbTiles(k), pr.mm
    parts.products(pe, pr)
    pe.wait_ge(s["h_ready"], KT * (u + 1))
    project(k, pe, pr, lambda t: z.h[:, t], KT, m=32)
    pe.wait_ge(s["mb_acum"], 1)
    for i, src in enumerate((z.dt, z.acum)):
        for b in range(2):
            mm(k.psum[:, 3, (2 * i + b) * 32:(2 * i + b + 1) * 32], src[:, b * P:(b + 1) * P],
               k.const("ident", 32)[:, 0:32], True, True, s["mb_cols"] if i and b else None)
    for i in range(8):
        quad, b = divmod(i, 2)
        pe.wait_ge(s["mb_silu"], 4 * quad + 4)
        if i >= 4:
            pe.wait_ge(s["mb_x_read"], i - 3)
        for n in range(4):
            pr.turn(k.psum[:, 4 + i % 4, n * P:(n + 1) * P], z.x[:, 4 * quad + n, b * P:(b + 1) * P],
                    s["mb_x_turned"] if n == 3 else None)
    for i in range(2):
        pe.wait_ge(s["mb_silu"], 24)
        pe.wait_ge(s["mb_x_read"], 5 + i)
        for n in range(4):
            pr.turn(k.psum[:, 4 + i, n * P:(n + 1) * P], z.b[:, 4 * i + n, 0:P],
                    s["mb_b_turned"] if n == 3 else None)
    pe.wait_ge(s["mb_silu"], 32)
    pe.wait_ge(s["mb_cols_read"], 1)
    pe.wait_ge(s["evacuated"], pr.q)

    def outputs(i):
        c, g = divmod(i, 8)
        b = i % 2
        pe.wait_ge(s["mb_mt"], i + 1)
        if i >= 2:
            pe.wait_ge(s["mb_y_read"], i - 1)
        else:
            pe.wait_ge(s["mb_x_read"], 8)
            pe.wait_ge(s["mb_b_read"], 2)
        if c:
            pe.wait_ge(s["mb_state_read"], 8)
        elif i >= 2:
            pe.wait_ge(s["mb_state_read"], i - 1)
        for n in range(4):
            head, rows = 4 * g + n, slice(64 * (n % 2), 64 * (n % 2) + 64)
            o = k.psum[rows, 4 + b, n // 2 * P:(n // 2 + 1) * P]
            last = n == 3 and c
            mm(o, z.xt[:, c, head], z.mt[b][:, n], True, not c)
            if c:
                mm(o, z.state[:, head], z.ce[b][:, n], False, True, s["mb_y"] if last else None)
        if not c:
            mm(k.psum[:, 6 + b, 0:T], z.bt[:, g], z.xd[b].rearrange("p h d -> p (h d)"), True, True, s["mb_y"])

    for i in range(MB_STEPS):
        c, g = divmod(i, 8)
        b = i % 2
        now = slice(c * P, (c + 1) * P)
        if i >= 2:
            pe.wait_ge(s["mb_masked"], i - 1)
            pe.wait_ge(s["mb_exp"], i - 1)
        mm(k.psum[:, b, 0:P], z.b[:, g, now], z.c[:, g, now], True, True, s["mb_cb"])
        for n in range(4):
            mm(k.psum[:, 2 + b, n * P:(n + 1) * P],
               k.const("ident", 32)[:, 4 * g + n:4 * g + n + 1].to_broadcast([32, P]), z.acum[:, now], True, True,
               s["mb_seg_sum"] if n == 3 else None)
        if i:
            outputs(i - 1)
    outputs(MB_STEPS - 1)
    for g in range(8):
        if g >= 4:
            pe.wait_ge(s["mb_rms"], g - 3)
        else:
            pe.wait_ge(s["mb_y_read"], MB_STEPS)
        for n in range(2):
            pe.wait_ge(s["mb_squares"], 2 * g + n + 1)
            mm(k.psum[:, 4 + g % 4, 0:T], k.const("ones"), z.sq[:, (2 * g + n) % 8], n == 0, n == 1,
               s["mb_group_sum"] if n else None)
    tail()
    output_products(k, pe, pr, 16, lambda t: z.x[:, t], lambda t: pe.wait_ge(s["mb_normed"], t + 1))


def mb_act(k, act, ev, parts):
    s, z, f, act_ = k.sem, MbTiles(k), ACT, k.nc.scalar.activation
    for m in range(16):
        ev.tile(z.z[:, m], f.Silu)
        parts.high(act, m + RING)
    for m in range(33):
        if m < 32:
            conv_act(k, act, ev.q, z.conv(m), ("mb_conv_w", "mb_conv_b"), m, 32)
            parts.high(act, 16 + m + RING)
            ev.q += 1
        if m:
            act.wait_ge(s["evacuated"], ev.q - (m < 32))
            act_(z.conv(m - 1), z.conv(m - 1), f.Silu).then_inc(s["mb_silu"], 1)
    ev.tile(z.dtx, f.Identity, m=32, bias=k.param("mb_dt_bias", rows=32))
    act_(z.neg_a, k.param("mb_A_log", rows=32), f.Exp).then_inc(s["mb_a"], 1)
    act.wait_ge(s["mb_dt_abs"], 1)
    act_(z.e32, z.e32, f.Exp, scale=-1.0).then_inc(s["mb_dt_exp"], 1)
    act.wait_ge(s["mb_cols"], 1)
    cols = k.psum[:, 3, 0:128].rearrange("p (w b h) -> p w b h", w=2, b=2)
    act_(z.cols[:, 0], cols[:, 0], f.Copy)
    act_(z.cols[:, 1], cols[:, 1], f.Copy, scale=-1.0).then_inc(s["mb_cols_read"], 1)
    for i in range(2):
        act.wait_ge(s["mb_b_turned"], i + 1)
        act_(z.bt[:, 4 * i:4 * i + 4], k.psum[:, 4 + i, :].rearrange("p (g n) -> p g n", g=4), f.Copy)\
            .then_inc(s["mb_b_read"], 1)

    def state(i):
        g, b = i % 8, i % 2
        act.wait_ge(s["mb_y"], i + 1)
        act_(z.state[:, 4 * g:4 * g + 4], k.psum[:, 6 + b, 0:T].rearrange("p (h d) -> p h d", h=4), f.Copy)\
            .then_inc(s["mb_state_read"], 1)

    for i in range(MB_STEPS):
        c, b = i // 8, i % 2
        act.wait_ge(s["mb_seg"], i + 1)
        ins = act_(z.e[b], z.e[b], f.Exp)
        if c:
            if i >= 2:
                act.wait_ge(s["mb_y"], i - 1)
            ins = act_(z.ce[b], k.psum[:, 2 + b, :].rearrange("p (h l) -> p h l", h=4), f.Exp)
        ins.then_inc(s["mb_exp"], 1)
        if 1 <= i <= 8:
            state(i - 1)
    for t in range(16):
        act.wait_ge(s["mb_gated"], t + 1)
        if t >= 8:
            act.wait_ge(s["mb_group_sum"], (t - 8) // 2 + 1)
        act_(z.sq[:, t % 8], z.x[:, t], f.Square).then_inc(s["mb_squares"], 1)
        if t % 2:
            g = t // 2
            act.wait_ge(s["mb_group_sum"], g + 1)
            if g >= 4:
                act.wait_ge(s["mb_normed"], 2 * (g - 3))
            act_(z.rms[g % 4], k.psum[:, 4 + g % 4, 0:T], f.Sqrt, bias=k.const("eps"), scale=1.0 / 256)\
                .then_inc(s["mb_rms"], 1)


def mb_vector(k, dve, own, u, q0, parts):
    s, z, v = k.sem, MbTiles(k), k.nc.vector
    mult, add = ALU.mult, ALU.add
    for m in range(15):
        parts.low(dve, m + RING)
    dve.wait_ge(s["evacuated"], q0 + 16)
    for m in range(32):
        parts.low(dve, 15 + m + RING)
        conv_vector(k, dve, own, q0 + 16 + m, z.conv(m), ("mb_conv_w", "mb_conv_b"), m, 32, m)
    dve.wait_ge(s["evacuated"], q0 + MB_TILES)
    v.scalar_tensor_tensor(z.e32, z.dtx, -1.0, z.dtx, mult, ALU.max).then_inc(s["mb_dt_abs"], 1)
    dve.wait_ge(s["mb_dt_exp"], 1)
    softplus_vector(k, own, z.dt, z.dtx, z.e32, z.z32, z.z32b)
    dve.wait_ge(s["mb_a"], 1)
    own.of(v.tensor_scalar(z.neg_a, z.neg_a, -1.0, None, mult))
    own.of(v.tensor_scalar(z.da, z.dt, z.neg_a, None, mult))
    v.tensor_tensor_scan(z.acum, k.const("ssd_reset", 32), z.da, 0.0, mult, add).then_inc(s["mb_acum"], 1)
    dve.wait_ge(s["mb_cols_read"], 1)
    for i in range(8):
        quad, b = divmod(i, 2)
        dve.wait_ge(s["mb_x_turned"], i + 1)
        v.tensor_tensor(z.xt[:, b, 8 * quad:8 * quad + 8],
                        k.psum[:, 4 + i % 4, :].rearrange("p (h d) -> p h d", h=8),
                        z.cols[:, 0, b, 8 * quad:8 * quad + 8].unsqueeze(2).to_broadcast([P, 8, 64]), mult)\
            .then_inc(s["mb_x_read"], 1)

    def outputs(i):
        c, g = divmod(i, 8)
        b, now = i % 2, slice(c * P, (c + 1) * P)
        dve.wait_ge(s["mb_y"], i + 1)
        for n in range(2):
            x = z.x[:, 2 * g + n, now]
            ins = v.scalar_tensor_tensor(x, x, k.param("mb_D", 2 * g + n), k.psum[:, 4 + b, n * P:(n + 1) * P],
                                         mult, add)
        ins.then_inc(s["mb_y_read"], 1)

    for i in range(MB_STEPS):
        c, g = divmod(i, 8)
        b, now = i % 2, slice(c * P, (c + 1) * P)
        heads = slice(4 * g, 4 * g + 4)
        dve.wait_ge(s["mb_seg_sum"], i + 1)
        if i >= 2:
            dve.wait_ge(s["mb_mt"], i - 1)
        for n in range(4):
            ins = v.scalar_tensor_tensor(z.e[b][:, n], k.psum[:, 2 + b, n * P:(n + 1) * P],
                                         z.cols[:, 1, c, 4 * g + n:4 * g + n + 1], k.const("ssd_open"), add, ALU.min)
        ins.then_inc(s["mb_seg"], 1)
        dve.wait_ge(s["mb_cb"], i + 1)
        v.tensor_tensor(z.cb[b], k.psum[:, b, 0:P], k.const("ssd_mask"), mult).then_inc(s["mb_masked"], 1)
        dve.wait_ge(s["mb_exp"], i + 1)
        dve.wait_ge(s["mb_masked"], i + 1)
        if i >= 2:
            dve.wait_ge(s["mb_y"], i - 1)
        v.tensor_tensor(z.mt[b], z.e[b], z.cb[b].unsqueeze(1).to_broadcast([P, 4, P]), mult)
        if c:
            ins = v.tensor_tensor(z.ce[b], z.ce[b], z.c[:, g, now].unsqueeze(1).to_broadcast([P, 4, P]), mult)
        else:
            ins = v.tensor_tensor(z.xd[b], z.xt[:, 0, heads], z.e[b][:, :, P - 1:P].to_broadcast([P, 4, 64]), mult)
        ins.then_inc(s["mb_mt"], 1)
        if i:
            outputs(i - 1)
    outputs(MB_STEPS - 1)
    dve.wait_ge(s["mb_y_read"], MB_STEPS)
    for t in range(16):
        v.tensor_tensor(z.x[:, t], z.x[:, t], z.z[:, t], mult).then_inc(s["mb_gated"], 1)
    for g in range(8):
        dve.wait_ge(s["mb_rms"], g + 1)
        own.of(v.reciprocal(z.rms[g % 4], z.rms[g % 4]))
        for n in range(2):
            t = 2 * g + n
            dve.wait_ge(s["mb_gated"], t + 1)
            dve.wait_ge(s["mb_squares"], t + 1)
            v.scalar_tensor_tensor(z.x[:, t], z.x[:, t], k.param("mb_norm_g", t), z.rms[g % 4], mult, mult)\
                .then_inc(s["mb_normed"], 1)



class Unit:

    def __init__(self, scores, masks, rows, values, out, bank, scale, sink=None):
        self.scores, self.masks, self.rows, self.values = scores, masks, rows, values
        self.out, self.bank, self.scale, self.sink = out, bank, scale, sink
        self.blocks = rows[-1][1] // P


class Attention:

    def __init__(self, k, units, at, base, base_outs):
        self.units, self.base, self.base_outs = units, base, base_outs
        self.p = [k.arena[:, int(at * 1024) + 768 * i:int(at * 1024) + 768 * (i + 1)] for i in range(2)]
        self.pt = [k.arena[:, int((at + 2) * 1024) + 768 * i:int((at + 2) * 1024) + 768 * (i + 1)]
                   for i in range(2)]
        self.stat = [k.small[:, 256 + 8 * i:264 + 8 * i] for i in range(2)]

    def outs_before(self, i):
        return self.base_outs + sum(u.out is not None for u in self.units[:i])


def attention_products(k, pe, pr, at):
    s, mm, b0 = k.sem, pr.mm, at.base
    for i in range(len(at.units) + 2):
        if i < len(at.units):
            if i >= 2:
                pe.wait_ge(s["at_added"], b0 + i - 1)
            u = at.units[i]
            for n, (bank, col, q, keys, width) in enumerate(u.scores):
                mm(k.psum[:, 2 * (i % 2) + bank, col:col + width], q, keys, True, True,
                   s["at_scored"] if n == len(u.scores) - 1 else None)
        if 1 <= i <= len(at.units):
            j = i - 1
            pe.wait_ge(s["at_prob"], b0 + j + 1)
            if j:
                pe.wait_ge(s["at_turned_read"], b0 + j)
            blocks = at.units[j].blocks
            for n in range(blocks):
                pr.turn(k.psum[:, 4 + n // 4, n % 4 * P:(n % 4 + 1) * P], at.p[j % 2][:, n * P:(n + 1) * P],
                        s["at_turned"] if n == blocks - 1 else None)
        if i >= 2:
            j = i - 2
            u = at.units[j]
            pe.wait_ge(s["at_turned_read"], b0 + j + 1)
            before = at.outs_before(j) - 1
            if before > at.base_outs:
                pe.wait_ge(s["at_out_read"], before)
            for m, (rows, col, parts) in enumerate(u.values):
                for n, (v, block) in enumerate(parts):
                    done = m == len(u.values) - 1 and n == len(parts) - 1
                    mm(k.psum[rows, 6 + u.bank, col:col + P], v, at.pt[j % 2][:, block * P:(block + 1) * P],
                       n == 0, n == len(parts) - 1, s["at_values"] if done else None)


def attention_act(k, act, at):
    s, act_, b0 = k.sem, k.nc.scalar.activation, at.base
    for i in range(len(at.units) + 2):
        if i < len(at.units):
            u, p, st = at.units[i], at.p[i % 2], at.stat[i % 2]
            act.wait_ge(s["at_max"], b0 + i + 1)
            for n, (a, b) in enumerate(u.rows):
                ins = act_(p[:, a:b], p[:, a:b], ACT.Exp, bias=st[:, 2 + n:3 + n], accum_out=st[:, 4 + n:5 + n])
            if u.sink is not None:
                ins = act_(st[:, 6:8], st[:, 2:4], ACT.Exp, bias=u.sink)
            ins.then_inc(s["at_exp"], 1)
        if 1 <= i <= len(at.units):
            j = i - 1
            act.wait_ge(s["at_turned"], b0 + j + 1)
            if j >= 2:
                act.wait_ge(s["at_values"], b0 + j - 1)
            width = at.units[j].blocks * P
            ins = act_(at.pt[j % 2][:, 0:min(width, 512)], k.psum[:, 4, 0:min(width, 512)], ACT.Copy)
            if width > 512:
                ins = act_(at.pt[j % 2][:, 512:width], k.psum[:, 5, 0:width - 512], ACT.Copy)
            ins.then_inc(s["at_turned_read"], 1)
        if i >= 2:
            u = at.units[i - 2]
            if u.out is not None:
                act.wait_ge(s["at_values"], b0 + i - 1)
                act_(u.out, k.psum[:, 6 + u.bank, 0:u.out.free_size()], ACT.Copy).then_inc(s["at_out_read"], 1)


def attention_vector(k, dve, own, at):
    s, v, b0 = k.sem, k.nc.vector, at.base
    for i in range(len(at.units) + 1):
        if i < len(at.units):
            u, p, st = at.units[i], at.p[i % 2], at.stat[i % 2]
            dve.wait_ge(s["at_scored"], b0 + i + 1)
            if i >= 2:
                dve.wait_ge(s["at_turned"], b0 + i - 1)
            for n, (bank, width, col, mask) in enumerate(u.masks):
                ins = v.scalar_tensor_tensor(p[:, col:col + width], k.psum[:, 2 * (i % 2) + bank, 0:width], u.scale,
                                             mask, ALU.mult, ALU.add)
                if n < len(u.masks) - 1:
                    own.mark(ins)
            ins.then_inc(s["at_added"], 1)
            own.wait()
            dve.wait_ge(s["at_added"], b0 + i + 1)
            for n, (a, b) in enumerate(u.rows):
                own.mark(v.tensor_reduce(st[:, n:n + 1], p[:, a:b], AX.X, ALU.max))
            own.wait()
            n = len(u.rows)
            v.tensor_scalar(st[:, 2:2 + n], st[:, 0:n], u.sink if u.sink is not None else -3e38, -1.0,
                            ALU.max, ALU.mult).then_inc(s["at_max"], 1)
        if i:
            u, p, st = at.units[i - 1], at.p[(i - 1) % 2], at.stat[(i - 1) % 2]
            dve.wait_ge(s["at_exp"], b0 + i)
            n = len(u.rows)
            if u.sink is not None:
                own.of(v.tensor_tensor(st[:, 4:4 + n], st[:, 4:4 + n], st[:, 6:6 + n], ALU.add))
            own.of(v.reciprocal(st[:, 4:4 + n], st[:, 4:4 + n]))
            for m, (a, b) in enumerate(u.rows):
                ins = v.tensor_scalar(p[:, a:b], p[:, a:b], st[:, 4 + m:5 + m], None, ALU.mult)
            ins.then_inc(s["at_prob"], 1)


def project_tokens(k, pe, pr, x, kt, width):
    if pr.q >= 2:
        pe.wait_ge(k.sem["evacuated"], pr.q + 1 - RING + 1)
    for t in range(kt):
        w = pr.take(width // P)
        for b in range(2):
            pr.mm(k.psum[:, (pr.q + b) % RING, 0:width], x(t)[:, b * P:(b + 1) * P], w, t == 0, t == kt - 1,
                  k.sem["projected"] if t == kt - 1 else None)
    pr.q += 2



SW_TILES = 12


class SwTiles:
    def __init__(self, k):
        self.h, self.q = k.tile(0), k.tile(2)
        self.k, self.v = k.tile(4, 2), k.tile(4.5, 2)
        self.sq = k.tile(5, 10)
        self.qz, self.kd, self.o = k.tile(8, 16), k.tile(12, 4), k.tile(20)
        units = []
        band = k.const("sw_band")
        for h in range(16):
            q, kd = self.qz[:, h], self.kd[:, h // 4]
            v = [self.v[:, b, 64 * (h // 4):64 * (h // 4) + 64] for b in range(2)]
            rows = slice(64 * (h % 2), 64 * (h % 2) + 64)
            units.append(Unit(
                scores=[(0, 0, q[:, 0:P], kd[:, 0:P], P), (0, P, q[:, P:T], kd[:, 0:T], T)],
                masks=[(0, 3 * P, 0, band)], rows=[(0, P), (P, 3 * P)],
                values=[(rows, 0, [(v[0], 0)]), (rows, P, [(v[0], 1), (v[1], 2)])],
                out=self.o[:, h // 2] if h % 2 else None, bank=h // 2 % 2, scale=64 ** -0.5,
                sink=k.param("sw_sinks", h)))
        self.attention = Attention(k, units, 14, 0, 0)


def sw_products(k, pe, pr, u, tail, parts):
    s, z, mm = k.sem, SwTiles(k), pr.mm
    parts.products(pe, pr)
    pe.wait_ge(s["h_ready"], KT * (u + 1))
    project_tokens(k, pe, pr, lambda t: z.h[:, t], KT, T)
    for t in range(10):
        pe.wait_ge(s["sw_squares"], t + 1)
        o = k.acc[:, t] if t < 8 else k.psum[:, 3, (t - 8) * T:(t - 7) * T]
        mm(o, k.const("head_ones"), z.sq[:, t], True, True, s["sw_head_sum"] if t % 2 else None)
    for j in range(4):
        pe.wait_ge(s["sw_k_normed"], 1)
        if j == 0:
            pe.wait_ge(s["sw_rms"], 5)
        mm(k.psum[:, 4 + j, 0:T], k.const(f"twice{j % 2}"), z.k[:, j // 2], True, True, s["sw_k_twice"])
    pe.wait_ge(s["sw_q_normed"], 1)
    pe.wait_ge(s["sw_k_twice_read"], 4)
    pe.wait_ge(s["evacuated"], pr.q)
    attention_products(k, pe, pr, z.attention)
    tail()
    output_products(k, pe, pr, KT, lambda t: z.o[:, t], lambda t: pe.wait_ge(s["at_out_read"], t + 1))


def sw_act(k, act, ev, parts):
    s, z, f, act_ = k.sem, SwTiles(k), ACT, k.nc.scalar.activation
    for m in range(10):
        dst = z.q[:, m] if m < 8 else z.k[:, m - 8]
        ev.tile(dst, f.Copy)
        parts.high(act, m + RING)
        act.wait_ge(s["evacuated"], ev.q)
        act_(z.sq[:, m], dst, f.Square).then_inc(s["sw_squares"], 1)
    for b in range(2):
        ev.tile(z.v[:, b], f.Copy)
    for n in range(5):
        act.wait_ge(s["sw_head_sum"], n + 1)
        src = k.acc[:, 2 * n:2 * n + 2] if n < 4 else k.psum[:, 3, :].rearrange("p (n t) -> p n t", n=2)
        act_(z.sq[:, 2 * n:2 * n + 2], src, f.Sqrt, bias=k.const("eps"), scale=1.0 / 64).then_inc(s["sw_rms"], 1)
    for j in range(4):
        act.wait_ge(s["sw_k_twice"], j + 1)
        act_(z.kd[:, j], k.psum[:, 4 + j, 0:T], f.Copy).then_inc(s["sw_k_twice_read"], 1)
    attention_act(k, act, z.attention)


def sw_vector(k, dve, own, u, q0, parts):
    s, z, v, mult = k.sem, SwTiles(k), k.nc.vector, ALU.mult
    for m in range(RING, parts.tiles):
        parts.low(dve, m)
    dve.wait_ge(s["evacuated"], q0 + 10)
    own.of(v.memset(z.qz, 0.0))
    dve.wait_ge(s["sw_rms"], 5)
    own.of(v.reciprocal(z.sq, z.sq))
    for t in range(2):
        ins = v.scalar_tensor_tensor(z.k[:, t], z.k[:, t], k.param("sw_k_norm"), z.sq[:, 8 + t], mult, mult)
    ins.then_inc(s["sw_k_normed"], 1)
    for t in range(KT):
        for i in range(2):
            r = slice(64 * i, 64 * i + 64)
            ins = v.scalar_tensor_tensor(z.qz[r, 2 * t + i], z.q[r, t], k.param("sw_q_norm")[r], z.sq[r, t],
                                         mult, mult)
    ins.then_inc(s["sw_q_normed"], 1)
    attention_vector(k, dve, own, z.attention)



LRU_C = 8.0
TWO_PI_PARTS = (6.28125, 0.0019340515136718750, 1.2555718421936e-06, -1.2154201256553e-10)
ROUND = 1.5 * 2.0 ** 23
PI_BELOW = 3.1415925
DH = 128


class B2Tiles:
    def __init__(self, k):
        self.h, self.q, self.k = k.tile(0), k.tile(2, 12), k.tile(5, 12)
        self.v = k.arena[:, 8 * 1024:11 * 1024].rearrange("p (b n) -> p b n", b=2)
        self.x, self.gelu, self.r, self.i = k.tile(11), k.tile(13), k.tile(15), k.tile(17)
        self.a, self.m, self.gates = k.tile(19), k.tile(21), k.tile(23, 16)
        self.o, self.mix, self.y = k.tile(19, 4), k.tile(20), k.tile(22, 3)
        self.cos, self.sin = k.rope[0:32, 0], k.rope[0:32, 1]
        self.lam = [k.small[:, 300 + 8 * i:308 + 8 * i] for i in range(5)]
        units = []
        for h in range(4):
            for b in range(2):
                w = P * (b + 1)
                now = slice(b * P, b * P + P)
                scores = [(g // 2, g % 2 * w, self.q[:, 4 * g + h, now], self.k[:, 4 * g + h, 0:w], w) if b else
                          (0, g * w, self.q[:, 4 * g + h, now], self.k[:, 4 * g + h, 0:w], w) for g in range(3)]
                bands = k.const("bands")
                masks = [(0, 512, 0, bands[:, 0:512]), (1, 256, 512, bands[:, 512:768])] if b else \
                    [(0, 384, 0, k.const("bands_first"))]
                parts = [(self.v[:, kb, (4 * g + h) * DH:(4 * g + h + 1) * DH], g * (b + 1) + kb)
                         for g in range(3) for kb in range(b + 1)]
                units.append(Unit(scores, masks, [(0, 3 * w)], [(slice(0, P), 0, parts)], self.o[:, h, now],
                                  (2 * h + b) % 2, DH ** -0.5))
        self.attention = Attention(k, units, 15, 16, 8)


def b2_products(k, pe, pr, parts):
    s, z, mm = k.sem, B2Tiles(k), pr.mm
    n = NORMS
    norm_products(k, pe, pr, n)

    def x(t):
        return z.h[:, t]
    parts.products(pe, pr)
    for m in range(3):
        project_tokens(k, pe, pr, x, KT, 512)
    for i in range(12):
        src = (z.q if i < 6 else z.k)[0:32, 2 * (i % 6):2 * (i % 6) + 2]
        if i >= 4:
            pe.wait_ge(s["b2_rotated_read"], i - 3)
        if i == 0:
            pe.wait_ge(s["evacuated"], pr.q - 6)
        mm(k.psum[0:32, 4 + i % 4, :], k.const("rotate", 32)[:, 0:32], src.rearrange("p n t -> p (n t)"), True, True,
           s["b2_rotated"])
    for m in range(16):
        if m == 0:
            pe.wait_ge(s["b2_convolved"], 1)
        project(k, pe, pr, lambda t: z.x[:, m % 8], 1)
    for m in range(16):
        project(k, pe, pr, x, KT)
    pe.wait_ge(s["b2_rope"], 12)
    pe.wait_ge(s["evacuated"], pr.q)
    pe.wait_ge(s["b2_lru"], KT)
    attention_products(k, pe, pr, z.attention)
    for m in range(KT):
        project(k, pe, pr, lambda t: z.x[:, t], KT)
    for m in range(KT):
        project(k, pe, pr, lambda t: z.o[:, t], 4,
                before=(lambda t: pe.wait_ge(s["at_out_read"], 8 + 2 * t + 2)) if m == 0 else None)
    output_products(k, pe, pr, KT, lambda t: z.mix[:, t], lambda t: pe.wait_ge(s["b2_mixed"], t + 1))
    norm_products(k, pe, pr, n + 1)
    norm_products(k, pe, pr, n + 2)
    k.h_at = KT * (n + 1)
    ffn_products(k, pe, pr, 2 * DEPTH)
    norm_products(k, pe, pr, n + 3)


def b2_act(k, act, ev, positions, parts):
    s, z, f, act_ = k.sem, B2Tiles(k), ACT, k.nc.scalar.activation
    n = NORMS
    act.wait_ge(s["mod_summed"], n)
    act.dma_start(k.rope[0:32, 2].bitcast(INT32), positions).then_inc(s["positions_loaded"], 16)
    norm_act(k, act, n, parts=parts)
    for m in range(KT):
        conv_act(k, act, ev.q + m, z.x[:, m], ("conv_w_2", "conv_b_2"), m, KT)
        parts.high(act, m + RING)
    ev.q += KT
    act.wait_ge(s["evacuated"], ev.q)
    for m in range(KT):
        ev.tile(z.gelu[:, m], f.Gelu_apprx_tanh)
        parts.high(act, KT + m + RING)
    for m in range(24):
        ev.tile((z.q if m < 12 else z.k)[:, m % 12], f.Copy)
        parts.high(act, 2 * KT + m + RING)
    for m in range(3):
        for b in range(2):
            ev.tile(z.v[:, b, 512 * m:512 * m + 512], f.Copy, width=512)
    act_(z.lam[1], k.param("lru_lambda_2", 0, KT), f.Abs).then_inc(s["act_own"], 1)
    act.wait_ge(s["act_own"], 1)
    act_(z.lam[1], z.lam[1], f.Exp, scale=-1.0).then_inc(s["b2_lam_exp"], 1)
    act.wait_ge(s["b2_angle"], 1)
    act_(k.rope[0:32, 0:2], k.rope[0:32, 0:2], f.Sin).then_inc(s["b2_sin"], 1)
    for m in range(16):
        ev.tile((z.r if m < 8 else z.i)[:, m % 8], f.Sigmoid, bias=k.param("b_rg_2" if m < 8 else "b_ig_2", m % 8))
    act.wait_ge(s["b2_lam"], 1)
    act.wait_ge(s["evacuated"], ev.q)
    for t in range(KT):
        act_(z.m[:, t], z.r[:, t], f.Tanh, scale=z.lam[0][:, t:t + 1]).then_inc(s["b2_tanh"], 1)
    for t in range(KT):
        act_(z.a[:, t], z.r[:, t], f.Exp, scale=z.lam[4][:, t:t + 1]).then_inc(s["b2_decay"], 1)
    for m in range(16):
        ev.tile(z.gates[:, m], f.Sigmoid)
    act.wait_ge(s["b2_power"], 1)
    act_(z.m, z.m, f.Sqrt, scale=2.0).then_inc(s["b2_root"], 1)
    attention_act(k, act, z.attention)
    ev.q += 2 * KT
    mixer = 4
    for t in range(KT):
        act.wait_ge(s["mixed"], KT // 2 * mixer + t // 2 + 1)
        act_(k.sq[:, t], k.acc[:, t], f.Square).then_inc(s["squares"], 1)
    norm_root(k, act, n + 1)
    norm_act(k, act, n + 2, ffn=2 * DEPTH)
    ffn_act(k, act, 2 * DEPTH)
    done = ffn_residual_wait(k, act, 2 * DEPTH)
    for t in range(KT):
        done(t)
        act_(k.sq[:, t], k.acc[:, t], f.Square).then_inc(s["squares"], 1)
    norm_root(k, act, n + 3)


def b2_vector(k, dve, own, q0, parts):
    s, z, v = k.sem, B2Tiles(k), k.nc.vector
    mult, add, sub = ALU.mult, ALU.add, ALU.subtract
    n = NORMS
    norm_vector(k, dve, own, n, k.param("pre_mix_norm_2", 0, KT), signal="h_ready", parts=parts)
    for m in range(KT):
        if m:
            parts.low(dve, m - 1 + RING)
        conv_vector(k, dve, own, q0 + m, z.x[:, m], ("conv_w_2", "conv_b_2"), m, KT, 32 + m)
    for m in range(KT - 1 + RING, parts.tiles):
        parts.low(dve, m)
    dve.wait_ge(s["positions_loaded"], 16)
    pos, ang, turns = k.rope[0:32, 2].bitcast(INT32), k.rope[0:32, 1], k.rope[0:32, 3]
    cos = k.rope[0:32, 0]
    own.of(v.tensor_copy(cos, pos))
    own.of(v.tensor_scalar(ang, cos, k.const("inv_freq", 32), None, mult))
    own.of(v.tensor_scalar(turns, ang, 1.0 / (2 * np.pi), None, mult))
    own.of(v.tensor_scalar(turns, turns, ROUND, None, add))
    own.of(v.tensor_scalar(turns, turns, ROUND, None, sub))
    for part in TWO_PI_PARTS:
        own.of(v.scalar_tensor_tensor(ang, turns, -part, ang, mult, add))
    own.of(v.tensor_scalar(cos, ang, np.pi / 2, None, add))
    own.of(v.tensor_scalar(turns, cos, np.pi, None, ALU.is_gt))
    own.of(v.scalar_tensor_tensor(cos, turns, -2 * np.pi, cos, mult, add))
    v.tensor_scalar(k.rope[0:32, 0:2], k.rope[0:32, 0:2], PI_BELOW, -PI_BELOW, ALU.min, ALU.max)\
        .then_inc(s["b2_angle"], 1)
    dve.wait_ge(s["evacuated"], q0 + KT)
    own.mark(v.tensor_scalar(z.lam[0], k.param("lru_lambda_2", 0, KT), -1.0, None, mult))
    v.tensor_copy(k.small[:, 104:105], k.const("eps")).then_inc(s["b2_convolved"], 1)
    own.wait()
    dve.wait_ge(s["b2_lam_exp"], 1)
    softplus_vector(k, own, z.lam[0], z.lam[0], z.lam[1], z.lam[2], z.lam[3])
    own.of(v.tensor_scalar(z.lam[0], z.lam[0], LRU_C, None, mult))
    v.tensor_scalar(z.lam[4], z.lam[0], -1.0, None, mult).then_inc(s["b2_lam"], 1)
    dve.wait_ge(s["b2_sin"], 1)
    for i in range(12):
        src = (z.q if i < 6 else z.k)[0:32, 2 * (i % 6):2 * (i % 6) + 2]
        dve.wait_ge(s["b2_rotated"], i + 1)
        own.of(v.tensor_tensor(src, src, z.cos.unsqueeze(1).to_broadcast([32, 2, T]), mult))
        tmp = k.rot_tmp[0:32]
        v.tensor_tensor(tmp, k.psum[0:32, 4 + i % 4, :].rearrange("p (n t) -> p n t", n=2),
                        z.sin.unsqueeze(1).to_broadcast([32, 2, T]), mult).then_inc(s["b2_rotated_read"], 1)
        dve.wait_ge(s["b2_rotated_read"], i + 1)
        v.tensor_tensor(src, src, tmp, add).then_inc(s["b2_rope"], 1)
        dve.wait_ge(s["b2_rope"], i + 1)
    dve.wait_ge(s["evacuated"], q0 + B2_GATED)
    own.of(v.tensor_tensor(z.x, z.x, z.i, mult))
    dve.wait_ge(s["b2_tanh"], KT)
    own.of(v.tensor_scalar(z.i, z.m, 1.0, None, add))
    own.of(v.reciprocal(z.i, z.i))
    v.tensor_tensor(z.m, z.m, z.i, mult).then_inc(s["b2_power"], 1)
    dve.wait_ge(s["b2_root"], 1)
    own.of(v.memset(z.m[:, :, 0:1], 1.0))
    own.of(v.tensor_tensor(z.x, z.x, z.m, mult))
    dve.wait_ge(s["b2_decay"], KT)
    for t in range(KT):
        own.of(v.tensor_tensor_scan(z.m[:, t], z.a[:, t], z.x[:, t], 0.0, mult, add))
        v.tensor_tensor(z.x[:, t], z.m[:, t], z.gelu[:, t], mult).then_inc(s["b2_lru"], 1)
    dve.wait_ge(s["b2_lru"], KT)
    attention_vector(k, dve, own, z.attention)
    q1 = q0 + B2_GATED + 16
    dve.wait_ge(s["evacuated"], q1)
    for m in range(KT):
        dve.wait_ge(s["projected"], q1 + m + 1)
        v.tensor_tensor(z.mix[:, m], z.gates[:, m], k.psum[:, (q1 + m) % RING, 0:T], mult)\
            .then_inc(s["evacuated"], 1)
    for m in range(KT):
        q = q1 + KT + m
        y = z.y[:, m % 2]
        dve.wait_ge(s["projected"], q + 1)
        if m >= 2:
            dve.wait_ge(s["b2_mixed"], m - 1)
        v.tensor_tensor(y, z.gates[:, KT + m], k.psum[:, q % RING, 0:T], mult).then_inc(s["evacuated"], 1)
        dve.wait_ge(s["evacuated"], q + 1)
        v.tensor_tensor(z.mix[:, m], z.mix[:, m], y, add).then_inc(s["b2_mixed"], 1)
    for i, name in enumerate(("post_mix_norm_2", "post_ffn_norm_2")):
        norm_vector(k, dve, own, n + 1 + 2 * i, k.param(name, 0, KT), src=k.acc, signal="normed")
        for t in range(KT):
            dve.wait_ge(s["normed"], KT * i + t + 1)
            v.tensor_tensor(k.x[:, t], k.x[:, t], k.h[:, t], add).then_inc(s["x_ready"], 1)
        if i == 0:
            if k.updates == 13:
                return
            dve.wait_ge(s["x_ready"], KT * 13)
            norm_vector(k, dve, own, n + 2, k.param("pre_ffn_norm_2", 0, KT), ffn=2 * DEPTH)
            ffn_vector(k, dve, 2 * DEPTH)


B2_GATED = 62
B2_TILES = B2_GATED + 32


SUBS = ["ffn", "rwkv", "ffn", "ffn", "mamba", "ffn", "ffn", "attention", "ffn", "ffn", "rwkv", "ffn"][:STAGES]
MIXER_SLOTS = {"rwkv": RW_SLOTS, "mamba": MB_SLOTS, "attention": SW_SLOTS, "ffn": FFN_SLOTS}
MIXER_TILES = {"rwkv": None, "mamba": MB_TILES, "attention": SW_TILES, "ffn": 0}


def plan():
    slot, q, ffns, mixers, out = 8, 0, 0, 0, []
    for kind in SUBS:
        number = ffns if kind == "ffn" else int(mixers > 0)
        out.append((kind, number, slot, q, mixers))
        slot += MIXER_SLOTS[kind]
        q += rw_tiles(number)["end"][0] if kind == "rwkv" else MIXER_TILES[kind]
        ffns, mixers = ffns + (kind == "ffn"), mixers + (kind != "ffn")
    return out, slot, q


def ffn_slot(i):
    subs, slots, _ = plan()
    starts = [slot for kind, _, slot, _, _ in subs if kind == "ffn"]
    return starts[i] if i < 2 * DEPTH else slots + B2_SLOTS


def build(nc, w, ada_w, consts, params, x_in, positions, out):
    ctx = ExitStack()
    k = Chip(nc)
    k.updates = UPDATES
    subs, slots, tiles = plan()
    v_first = nc.dram_tensor("v_first", (P, KT, T), FP32, kind="Internal").ap()
    with ctx:
        layout(k, ctx)
        block = ctx.enter_context(nc.Block())
        sem = k.sem
        parts = {kind: Parts(k, ("mamba", "attention").index(kind), slot, q)
                 for kind, _, slot, q, _ in subs if kind in ("mamba", "attention")}
        second_parts = Parts(k, 2, slots, tiles)

        @block.sync
        def _(sp):
            sp.dma_start(k.params[:, :], params).then_inc(sem["inputs_loaded"], 16)
            sp.dma_start(k.x[:, :, :], x_in).then_inc(sem["inputs_loaded"], 16)
            sp.dma_start(k.consts[:, :], consts).then_inc(sem["inputs_loaded"], 16)
            stream_weights(k, sp, w, -(-(slots + B2_TOTAL) // RING) * RING)
            sp.wait_ge(sem["x_ready"], KT * UPDATES)
            sp.dma_start(out, k.x[:, :, :]).then_inc(sem["stored"], 16)
            sp.wait_ge(sem["stored"], 16)

        @block.gpsimd
        def _(pool):
            ada_sums(k, pool, ada_w, len(subs) - 1)

        @block.scalar
        def _(act):
            ev = Evacuation(k, act)
            act.wait_ge(sem["inputs_loaded"], 48)
            nc.scalar.activation(k.c_act[:, :], k.param("c", 0, KT), ACT.Silu).then_inc(sem["c_silu"], 1)
            for u, (kind, n, slot, q, m) in enumerate(subs):
                norm_act(k, act, u, shift=k.mod[:, u % 2, 0:8], ffn=n if kind == "ffn" else None,
                         parts=parts.get(kind))
                if kind == "ffn":
                    ffn_act(k, act, n)
                elif kind == "rwkv":
                    rw_act(k, act, ev, n, v_first)
                elif kind == "mamba":
                    mb_act(k, act, ev, parts["mamba"])
                else:
                    sw_act(k, act, ev, parts["attention"])
                assert ev.q == (subs[u + 1][3] if u + 1 < len(subs) else tiles)
            if B2_TOTAL:
                b2_act(k, act, ev, positions, second_parts)

        @block.vector
        def _(dve):
            own = Own(dve, sem["dve_own"])
            own.of(nc.vector.memset(k.c_pick, 0.0))
            dve.wait_ge(sem["c_silu"], 1)
            nc.vector.tensor_copy(k.c_pick[:, :, 23], k.c_act[:, :]).then_inc(sem["c_ready"], 1)
            dve.wait_ge(sem["inputs_loaded"], 48)
            mod_vector(k, dve, own, 0)
            for u, (kind, n, slot, q, m) in enumerate(subs):
                norm_vector(k, dve, own, u, k.gain[:, u % 2, :], shift=k.mod[:, u % 2, 0:8],
                            ffn=n if kind == "ffn" else None, parts=parts.get(kind))
                if kind == "ffn":
                    ffn_vector(k, dve, n)
                elif kind == "rwkv":
                    rw_vector(k, dve, own, u, n, q)
                elif kind == "mamba":
                    mb_vector(k, dve, own, u, q, parts["mamba"])
                else:
                    sw_vector(k, dve, own, u, q, parts["attention"])
                if u + 1 < len(subs):
                    mod_vector(k, dve, own, u + 1)
                if kind == "ffn":
                    residual(k, dve, u, k.half_gate[:, u % 2, :], ffn_residual_wait(k, dve, n))
                else:
                    residual(k, dve, u, k.mod[:, u % 2, 16:24], mixed_wait(k, dve, m))
            if B2_TOTAL:
                b2_vector(k, dve, own, tiles, second_parts)

        @block.tensor
        def _(pe):
            pr = Products(k, pe)
            pe.wait_ge(sem["inputs_loaded"], 48)
            first_mod_products(k, pe, pr)
            pr.align()
            for u, (kind, n, slot, q, m) in enumerate(subs):
                assert pr.slot == slot and pr.q == q
                k.h_at = KT * u
                norm_products(k, pe, pr, u)

                def tail():
                    if u + 1 < len(subs):
                        mod_products(k, pe, pr, u + 1)
                if kind == "ffn":
                    ffn_products(k, pe, pr, n, tail)
                elif kind == "rwkv":
                    rw_products(k, pe, pr, n, u, tail)
                elif kind == "mamba":
                    mb_products(k, pe, pr, u, tail, parts["mamba"])
                else:
                    sw_products(k, pe, pr, u, tail, parts["attention"])
            if B2_TOTAL:
                b2_products(k, pe, pr, second_parts)


def kernel(**inputs):
    import concourse.bacc as bacc
    from concourse.bass_utils import run_bass_kernel_spmd

    v = {n: np.asarray(a) for n, a in inputs.items()}
    parts = param_parts(v)
    ada = v["ada_w"].reshape(DEPTH, KT, P, ADA_STEPS * 3, ADA_CHUNK).transpose(0, 3, 2, 1, 4)
    ada = ada.reshape(NORMS * ADA_STEPS, P, KT, ADA_CHUNK)
    arrays = {
        "weights": weight_slots(v),
        "ada_w": np.concatenate([ada[ADA_STEPS:], np.zeros_like(ada[:2])]),
        "consts": np.concatenate(list(CONST_PARTS.values()), 1),
        "params": np.concatenate([parts[n] for n, _ in PARAM_WIDTHS], 1),
        "x": v["x"][0].T.reshape(KT, P, T).transpose(1, 0, 2),
        "positions": np.tile(v["positions_2"], (32, 1)),
    }
    arrays = {n: np.ascontiguousarray(a) for n, a in arrays.items()}
    nc = bacc.Bacc("TRN2", target_bir_lowering=False, num_devices=1)
    args = [nc.dram_tensor("in_" + n, a.shape, mybir.dt.from_np(a.dtype), kind="ExternalInput").ap()
            for n, a in arrays.items()]
    out = nc.dram_tensor("out", (P, KT, T), FP32, kind="ExternalOutput").ap()
    build(nc, *args, out)
    r = run_bass_kernel_spmd(nc, [{"in_" + n: a for n, a in arrays.items()}], core_ids=[0])
    y = r.results[0]["out"]
    return np.ascontiguousarray(y.transpose(1, 0, 2).reshape(D, T).T)[None]
```
